# Optimizing a Trainium2 kernel written in Bass

```python
import math
import jax
import jax.numpy as jnp
from jax import lax
import numpy as np

D_MODEL = 1024
BATCH = 1
SEQ = 256
DEPTH = 2

MEM_LEN = 256
HEAD_DIM = 64
ROPE_THETA = 500000.0
ROPE_DIM = HEAD_DIM // 4
NORM_EPS = 1e-5

POOL_WINDOWS = (2, 4, 8, 16)
POOL_GROUPS = 4
POOL_GROUP_DIM = D_MODEL // 16
POOL_DIM = POOL_GROUPS * POOL_GROUP_DIM
MOBA_HEADS = (D_MODEL - POOL_DIM) // HEAD_DIM
MOBA_DIM = MOBA_HEADS * HEAD_DIM
MOBA_BLOCK = 256
MOBA_TOPK = 3
MOBA_QC = 16
AB_IN = POOL_DIM + 3 * MOBA_DIM
NSA_HEADS = D_MODEL // HEAD_DIM
NSA_GROUPS = 4
NSA_HPG = NSA_HEADS // NSA_GROUPS
NSA_KV_DIM = NSA_GROUPS * HEAD_DIM
CMP_LEN = 32
CMP_STRIDE = 16
CMP_HIDDEN = 4 * HEAD_DIM
SLC_BLOCK = 64
SLC_TOPN = 16
WINDOW = 512
NSA_QC = 32
FORCE_SCORE = 1e4
C_IN = NSA_HEADS * HEAD_DIM + 6 * NSA_KV_DIM + 3 * NSA_HEADS
XA_HEADS = 4
XA_DIM = XA_HEADS * HEAD_DIM
D_FF = 2816
N_EXPERTS = 8
TOP_K = 2
D_FF_EXPERT = 3584
N_EVEN = (DEPTH + 1) // 2
N_ODD = DEPTH // 2

kernel_name = 'hybrid_pool_moba_nsa_moe_decoder'

def rmsnorm(x, g):
    xf = x.astype(jnp.float32)
    y = xf * lax.rsqrt(jnp.mean(xf * xf, axis=-1, keepdims=True) + NORM_EPS)
    return y.astype(x.dtype) * g

def rope_tables(positions):
    inv = ROPE_THETA ** (-jnp.arange(0, ROPE_DIM, 2, dtype=jnp.float32) / ROPE_DIM)
    ang = positions.astype(jnp.float32)[:, None] * inv[None, :]
    return jnp.cos(ang), jnp.sin(ang)

def apply_rope(x, cos, sin):
    xr, xp = x[..., :ROPE_DIM], x[..., ROPE_DIM:]
    x1, x2 = xr[..., :ROPE_DIM // 2], xr[..., ROPE_DIM // 2:]
    c = cos[None, :, None, :].astype(x.dtype)
    s = sin[None, :, None, :].astype(x.dtype)
    return jnp.concatenate([x1 * c - x2 * s, x1 * s + x2 * c, xp], axis=-1)

def masked_softmax(s, mask):
    s = jnp.where(mask, s.astype(jnp.float32), -jnp.inf)
    m = jnp.max(s, axis=-1, keepdims=True)
    m = jnp.where(jnp.isfinite(m), m, 0.0)
    e = jnp.where(mask, jnp.exp(s - m), 0.0)
    return e / jnp.maximum(jnp.sum(e, axis=-1, keepdims=True), 1e-30)

def gather_blocks(blocks, idx):
    return jax.vmap(jax.vmap(lambda bl, ix: bl[ix]))(blocks, idx)

def swiglu(h, wg, wu, wd):
    return (jax.nn.silu(h @ wg) * (h @ wu)) @ wd

def pool_mixer(u, pool_w, pool_scale):
    B_, S_, _ = u.shape
    uf = u.astype(jnp.float32)
    cs = jnp.concatenate([jnp.zeros((B_, 1, POOL_DIM), jnp.float32), jnp.cumsum(uf, axis=1)], axis=1)
    t = jnp.arange(S_)
    outs = []
    for g, w in enumerate(POOL_WINDOWS):
        sl = slice(g * POOL_GROUP_DIM, (g + 1) * POOL_GROUP_DIM)
        start = jnp.maximum(t + 1 - w, 0)
        cnt = jnp.minimum(t + 1, w).astype(jnp.float32)
        outs.append((cs[:, t + 1, sl] - cs[:, start, sl]) / cnt[None, :, None])
    pooled = (jnp.concatenate(outs, axis=-1) - uf).astype(u.dtype)
    pg = pooled.reshape(B_, S_, POOL_GROUPS, POOL_GROUP_DIM)
    y = jnp.einsum('bsgc,gcd->bsgd', pg, pool_w).reshape(B_, S_, POOL_DIM)
    return y * pool_scale

def moba_attention(q, k, v):
    B_, S_, H, dh = q.shape
    nb = -(-S_ // MOBA_BLOCK)
    s_pad = nb * MOBA_BLOCK
    pad = ((0, 0), (0, s_pad - S_), (0, 0), (0, 0))
    kb = jnp.pad(k, pad).transpose(0, 2, 1, 3).reshape(B_, H, nb, MOBA_BLOCK, dh)
    vb = jnp.pad(v, pad).transpose(0, 2, 1, 3).reshape(B_, H, nb, MOBA_BLOCK, dh)
    kmean = jnp.mean(kb.astype(jnp.float32), axis=3)
    qh = q.transpose(0, 2, 1, 3)
    scale = dh ** -0.5
    topk = min(MOBA_TOPK, nb - 1)

    def chunk(c):
        s0 = c * MOBA_QC
        tq = s0 + jnp.arange(MOBA_QC)
        qc = lax.dynamic_slice_in_dim(qh, s0, MOBA_QC, axis=2)
        blk = s0 // MOBA_BLOCK
        k_own = lax.dynamic_slice_in_dim(kb, blk, 1, axis=2)[:, :, 0]
        v_own = lax.dynamic_slice_in_dim(vb, blk, 1, axis=2)[:, :, 0]
        pos_own = blk * MOBA_BLOCK + jnp.arange(MOBA_BLOCK)
        m_own = (pos_own[None, :] <= tq[:, None])[None, None]
        s_own = jnp.einsum('bhqd,bhkd->bhqk', qc, k_own) * scale
        if topk == 0:
            p = masked_softmax(s_own, m_own).astype(v.dtype)
            return jnp.einsum('bhqk,bhkd->bhqd', p, v_own)
        gate = jnp.einsum('bhqd,bhnd->bhqn', qc.astype(jnp.float32), kmean)
        gate = jnp.where(jnp.arange(nb) < blk, gate, -jnp.inf)
        _, idx = lax.top_k(gate, topk)
        sel_ok = idx < blk
        k_sel = gather_blocks(kb, idx)
        v_sel = gather_blocks(vb, idx)
        s_sel = jnp.einsum('bhqd,bhqnkd->bhqnk', qc, k_sel).reshape(B_, H, MOBA_QC, topk * MOBA_BLOCK) * scale
        m_sel = jnp.repeat(sel_ok, MOBA_BLOCK, axis=-1)
        m_all = jnp.concatenate([m_sel, jnp.broadcast_to(m_own, (B_, H, MOBA_QC, MOBA_BLOCK))], axis=-1)
        p = masked_softmax(jnp.concatenate([s_sel, s_own], axis=-1), m_all).astype(v.dtype)
        p_sel = p[..., :topk * MOBA_BLOCK].reshape(B_, H, MOBA_QC, topk, MOBA_BLOCK)
        p_own = p[..., topk * MOBA_BLOCK:]
        return (jnp.einsum('bhqnk,bhqnkd->bhqd', p_sel, v_sel)
                + jnp.einsum('bhqk,bhkd->bhqd', p_own, v_own))

    out = lax.map(chunk, jnp.arange(S_ // MOBA_QC))
    return out.transpose(1, 0, 3, 2, 4).reshape(B_, S_, H * dh)

def pool_moba_mixer(h, w_in, pool_w, pool_scale, w_out, cos, sin):
    B_, S_, _ = h.shape
    u = h @ w_in
    u_pool, q, k, v = jnp.split(u, [POOL_DIM, POOL_DIM + MOBA_DIM, POOL_DIM + 2 * MOBA_DIM], axis=-1)
    shp = (B_, S_, MOBA_HEADS, HEAD_DIM)
    q = apply_rope(q.reshape(shp), cos, sin)
    k = apply_rope(k.reshape(shp), cos, sin)
    y_a = pool_mixer(u_pool, pool_w, pool_scale)
    y_b = moba_attention(q, k, v.reshape(shp))
    return jnp.concatenate([y_a, y_b], axis=-1) @ w_out

def compress_blocks(t, pe, w1, w2):
    B_, S_, G, dh = t.shape
    n_cmp = (S_ - CMP_LEN) // CMP_STRIDE + 1
    idx = np.arange(n_cmp)[:, None] * CMP_STRIDE + np.arange(CMP_LEN)[None, :]
    blk = t[:, idx] + pe[None, None, :, None, :]
    flat = blk.transpose(0, 1, 3, 2, 4).reshape(B_, n_cmp, G, CMP_LEN * dh)
    return jax.nn.gelu(flat @ w1) @ w2

def nsa_mixer(h, w_in, pe_k, pe_v, k_w1, k_w2, v_w1, v_w2, w_out, cos, sin):
    B_, S_, _ = h.shape
    G, HPG, dh = NSA_GROUPS, NSA_HPG, HEAD_DIM
    u = h @ w_in
    qd = NSA_HEADS * dh
    offs = [qd + i * NSA_KV_DIM for i in range(1, 7)]
    q, kc, vc, ks, vs, kw, vw, gl = jnp.split(u, [qd] + offs, axis=-1)
    q = q.reshape(B_, S_, NSA_HEADS, dh)
    kvs = (B_, S_, G, dh)
    kc, vc, ks, vs, kw, vw = [a.reshape(kvs) for a in (kc, vc, ks, vs, kw, vw)]
    gates = jax.nn.sigmoid(gl.reshape(B_, S_, NSA_HEADS, 3).astype(jnp.float32)).astype(h.dtype)
    q_rot = apply_rope(q, cos, sin).reshape(B_, S_, G, HPG, dh)
    ks = apply_rope(ks, cos, sin)
    kw = apply_rope(kw, cos, sin)
    q_cmp = q.reshape(B_, S_, G, HPG, dh)
    scale = dh ** -0.5
    t = jnp.arange(S_)

    k_cmp = compress_blocks(kc, pe_k, k_w1, k_w2)
    v_cmp = compress_blocks(vc, pe_v, v_w1, v_w2)
    n_cmp = k_cmp.shape[1]
    cmp_end = jnp.arange(n_cmp) * CMP_STRIDE + CMP_LEN - 1
    m_cmp = cmp_end[None, :] <= t[:, None]
    s_cmp = jnp.einsum('bsghd,bngd->bghsn', q_cmp, k_cmp) * scale
    p_cmp = masked_softmax(s_cmp, m_cmp)
    o_cmp = jnp.einsum('bghsn,bngd->bsghd', p_cmp.astype(v_cmp.dtype), v_cmp).reshape(B_, S_, NSA_HEADS, dh)

    n_slc = -(-S_ // SLC_BLOCK)
    c_s = np.arange(n_cmp) * CMP_STRIDE
    s_s = np.arange(n_slc) * SLC_BLOCK
    ov = np.clip(np.minimum(c_s[:, None] + CMP_LEN, s_s[None, :] + SLC_BLOCK) - np.maximum(c_s[:, None], s_s[None, :]), 0, None) / CMP_LEN
    p_slc = jnp.einsum('bgsn,nj->bgsj', jnp.sum(p_cmp, axis=2), jnp.asarray(ov, jnp.float32))
    t_blk = t // SLC_BLOCK
    j = jnp.arange(n_slc)
    forced = (j[None, :] == 0) | (j[None, :] == t_blk[:, None]) | (j[None, :] == t_blk[:, None] - 1)
    valid = j[None, :] <= t_blk[:, None]
    score = jnp.where(valid, jnp.where(forced, FORCE_SCORE, p_slc), -1.0)
    top_n = min(SLC_TOPN, n_slc)
    _, sel_idx = lax.top_k(score, top_n)

    kbs = ks.transpose(0, 2, 1, 3).reshape(B_, G, n_slc, SLC_BLOCK, dh)
    vbs = vs.transpose(0, 2, 1, 3).reshape(B_, G, n_slc, SLC_BLOCK, dh)
    wpad = ((0, 0), (WINDOW, 0), (0, 0), (0, 0))
    kwp = jnp.pad(kw, wpad)
    vwp = jnp.pad(vw, wpad)

    def chunk(c):
        s0 = c * NSA_QC
        tq = s0 + jnp.arange(NSA_QC)
        qc = lax.dynamic_slice_in_dim(q_rot, s0, NSA_QC, axis=1)
        ic = lax.dynamic_slice_in_dim(sel_idx, s0, NSA_QC, axis=2)
        k_sel = gather_blocks(kbs, ic)
        v_sel = gather_blocks(vbs, ic)
        s_sel = jnp.einsum('bqghd,bgqnkd->bghqnk', qc, k_sel).reshape(B_, G, HPG, NSA_QC, top_n * SLC_BLOCK) * scale
        kpos = ic[..., None] * SLC_BLOCK + jnp.arange(SLC_BLOCK)
        m_sel = (kpos <= tq[None, None, :, None, None]) & (ic <= (tq // SLC_BLOCK)[None, None, :, None])[..., None]
        m_sel = m_sel.reshape(B_, G, NSA_QC, top_n * SLC_BLOCK)[:, :, None]
        p_sel = masked_softmax(s_sel, m_sel).astype(v_sel.dtype).reshape(B_, G, HPG, NSA_QC, top_n, SLC_BLOCK)
        o_sel = jnp.einsum('bghqnk,bgqnkd->bqghd', p_sel, v_sel)
        kwc = lax.dynamic_slice_in_dim(kwp, s0, NSA_QC + WINDOW, axis=1)
        vwc = lax.dynamic_slice_in_dim(vwp, s0, NSA_QC + WINDOW, axis=1)
        kp = s0 - WINDOW + jnp.arange(NSA_QC + WINDOW)
        m_win = (kp[None, :] >= 0) & (kp[None, :] <= tq[:, None]) & (tq[:, None] - kp[None, :] < WINDOW)
        s_win = jnp.einsum('bqghd,bkgd->bghqk', qc, kwc) * scale
        p_win = masked_softmax(s_win, m_win).astype(vwc.dtype)
        o_win = jnp.einsum('bghqk,bkgd->bqghd', p_win, vwc)
        return o_sel, o_win

    o_sel, o_win = lax.map(chunk, jnp.arange(S_ // NSA_QC))
    o_sel = o_sel.transpose(1, 0, 2, 3, 4, 5).reshape(B_, S_, NSA_HEADS, dh)
    o_win = o_win.transpose(1, 0, 2, 3, 4, 5).reshape(B_, S_, NSA_HEADS, dh)
    y = gates[..., 0:1] * o_cmp + gates[..., 1:2] * o_sel + gates[..., 2:3] * o_win
    return y.reshape(B_, S_, NSA_HEADS * dh) @ w_out

def memory_cross_attention(h, mem_n, wq, wkv, wo):
    B_, S_, _ = h.shape
    q = (h @ wq).reshape(B_, S_, XA_HEADS, HEAD_DIM)
    k, v = jnp.split(mem_n @ wkv, 2, axis=-1)
    k = k.reshape(B_, MEM_LEN, XA_HEADS, HEAD_DIM)
    v = v.reshape(B_, MEM_LEN, XA_HEADS, HEAD_DIM)
    s = jnp.einsum('bshd,bmhd->bhsm', q, k) * (HEAD_DIM ** -0.5)
    p = jax.nn.softmax(s.astype(jnp.float32), axis=-1).astype(v.dtype)
    o = jnp.einsum('bhsm,bmhd->bshd', p, v).reshape(B_, S_, XA_DIM)
    return o @ wo

def moe_swiglu(h, router_w, wg, wu, wd):
    logits = (h @ router_w).astype(jnp.float32)
    top_val, top_idx = lax.top_k(logits, TOP_K)
    w = jax.nn.softmax(top_val, axis=-1)
    gate = jnp.sum(jax.nn.one_hot(top_idx, N_EXPERTS, dtype=jnp.float32) * w[..., None], axis=-2).astype(h.dtype)
    out = jnp.zeros_like(h)
    for e in range(N_EXPERTS):
        out = out + gate[..., e:e + 1] * swiglu(h, wg[e], wu[e], wd[e])
    return out

def setup_inputs(seed: int = 0) -> dict:
    key = jax.random.key(seed)
    ks = jax.random.split(key, 28)
    D = D_MODEL
    f32 = jnp.float32

    def nrm(k, shape, fan_in):
        return jax.random.normal(k, shape, f32) * (fan_in ** -0.5)

    return {
        'x': jax.random.normal(ks[0], (BATCH, SEQ, D), f32),
        'mem': jax.random.normal(ks[1], (BATCH, MEM_LEN, D), f32),
        'positions': jnp.arange(SEQ, dtype=jnp.int32),
        'norm_g': 1.0 + 0.02 * jax.random.normal(ks[2], (DEPTH, 3, D), f32),
        'mem_g': 1.0 + 0.02 * jax.random.normal(ks[3], (D,), f32),
        'final_g': 1.0 + 0.02 * jax.random.normal(ks[4], (D,), f32),
        'w_in_ab': nrm(ks[5], (N_EVEN, D, AB_IN), D),
        'pool_w': nrm(ks[6], (N_EVEN, POOL_GROUPS, POOL_GROUP_DIM, POOL_GROUP_DIM), POOL_GROUP_DIM),
        'pool_scale': 1.0 + 0.1 * jax.random.normal(ks[7], (N_EVEN, POOL_DIM), f32),
        'w_out_ab': nrm(ks[8], (N_EVEN, D, D), D),
        'ffn_w_gate': nrm(ks[9], (N_EVEN, D, D_FF), D),
        'ffn_w_up': nrm(ks[10], (N_EVEN, D, D_FF), D),
        'ffn_w_down': nrm(ks[11], (N_EVEN, D_FF, D), D_FF),
        'w_in_c': nrm(ks[12], (N_ODD, D, C_IN), D),
        'cmp_pe_k': 0.1 * jax.random.normal(ks[13], (N_ODD, CMP_LEN, HEAD_DIM), f32),
        'cmp_pe_v': 0.1 * jax.random.normal(ks[14], (N_ODD, CMP_LEN, HEAD_DIM), f32),
        'cmp_k_w1': nrm(ks[15], (N_ODD, CMP_LEN * HEAD_DIM, CMP_HIDDEN), CMP_LEN * HEAD_DIM),
        'cmp_k_w2': nrm(ks[16], (N_ODD, CMP_HIDDEN, HEAD_DIM), CMP_HIDDEN),
        'cmp_v_w1': nrm(ks[17], (N_ODD, CMP_LEN * HEAD_DIM, CMP_HIDDEN), CMP_LEN * HEAD_DIM),
        'cmp_v_w2': nrm(ks[18], (N_ODD, CMP_HIDDEN, HEAD_DIM), CMP_HIDDEN),
        'w_out_c': nrm(ks[19], (N_ODD, D, D), D),
        'router_w': nrm(ks[20], (N_ODD, D, N_EXPERTS), D),
        'moe_w_gate': nrm(ks[21], (N_ODD, N_EXPERTS, D, D_FF_EXPERT), D),
        'moe_w_up': nrm(ks[22], (N_ODD, N_EXPERTS, D, D_FF_EXPERT), D),
        'moe_w_down': nrm(ks[23], (N_ODD, N_EXPERTS, D_FF_EXPERT, D), D_FF_EXPERT),
        'xa_wq': nrm(ks[24], (DEPTH, D, XA_DIM), D),
        'xa_wkv': nrm(ks[25], (DEPTH, D, 2 * XA_DIM), D),
        'xa_wo': nrm(ks[26], (DEPTH, XA_DIM, D), XA_DIM),
    }

def reference(x, mem, positions, norm_g, mem_g, final_g, w_in_ab, pool_w, pool_scale, w_out_ab,
              ffn_w_gate, ffn_w_up, ffn_w_down, w_in_c, cmp_pe_k, cmp_pe_v, cmp_k_w1, cmp_k_w2,
              cmp_v_w1, cmp_v_w2, w_out_c, router_w, moe_w_gate, moe_w_up, moe_w_down,
              xa_wq, xa_wkv, xa_wo):
    cos, sin = rope_tables(positions)
    mem_n = rmsnorm(mem, mem_g)
    for layer in range(DEPTH):
        i = layer // 2
        h = rmsnorm(x, norm_g[layer, 0])
        if layer % 2 == 0:
            x = x + pool_moba_mixer(h, w_in_ab[i], pool_w[i], pool_scale[i], w_out_ab[i], cos, sin)
        else:
            x = x + nsa_mixer(h, w_in_c[i], cmp_pe_k[i], cmp_pe_v[i], cmp_k_w1[i], cmp_k_w2[i],
                              cmp_v_w1[i], cmp_v_w2[i], w_out_c[i], cos, sin)
        h = rmsnorm(x, norm_g[layer, 1])
        x = x + memory_cross_attention(h, mem_n, xa_wq[layer], xa_wkv[layer], xa_wo[layer])
        h = rmsnorm(x, norm_g[layer, 2])
        if layer % 2 == 0:
            x = x + swiglu(h, ffn_w_gate[i], ffn_w_up[i], ffn_w_down[i])
        else:
            x = x + moe_swiglu(h, router_w[i], moe_w_gate[i], moe_w_up[i], moe_w_down[i])
    return rmsnorm(x, final_g)


_drawn_inputs = setup_inputs


def setup_inputs(seed=0):
    import zlib

    import numpy as np

    out = dict(_drawn_inputs(seed))
    spreads = {}
    factors = {'mem_g': 2.814, 'final_g': 2.873, 'cmp_pe_k': 8.0}
    for name, (base, spread) in spreads.items():
        noise = np.random.default_rng([zlib.crc32(name.encode()), seed]).standard_normal(out[name].shape)
        drawn = base * np.exp(spread * noise) if base else spread * noise
        out[name] = jnp.asarray(drawn.astype(out[name].dtype))
    for name, factor in factors.items():
        out[name] = (out[name] * factor).astype(out[name].dtype)
    return out
```

```python
import math
from contextlib import ExitStack, contextmanager

import numpy as np

import concourse.bass as bass
from concourse import mybir

F32 = mybir.dt.float32
BF16 = mybir.dt.bfloat16
I32 = mybir.dt.int32
U32 = mybir.dt.uint32
ALU = mybir.AluOpType
ACT = mybir.ActivationFunctionType
AX = mybir.AxisListType.X

P = 128
D = 1024
S = 256
TT = S // P
KD = D // P
DH = 64
ROPE = 16
HALF = ROPE // 2
THETA = 500000.0
EPS = 1e-5
WINDOWS = (2, 4, 8, 16)
POOL = 256
MOBA = D - POOL
MOBA_UNITS = MOBA // 256
GROUPS = 4
CMP_LEN, CMP_STRIDE = 32, 16
NCMP = (S - CMP_LEN) // CMP_STRIDE + 1
CMP_HID = 256
KV = 256
C_IN = D + 6 * KV + 48
FF = 2816
FSTEP = 256
FSTEPS = FF // FSTEP
NE = 8
FFE = 3584
ESTEP = 512
ESTEPS = FFE // ESTEP
RING = 7
SLOT = 4096
BIG = 1e30
CLAMP = 1e20
SCALE = DH ** -0.5
MAGIC = 1.5 * 2.0 ** 23
TWO_PI = (6.25, 0.03125, 63.0 / 32768.0)
TWO_PI_REST = 2 * math.pi - sum(TWO_PI)
KC0, VC0, KS0, VS0, KW0, VW0, GL0 = (D + i * KV for i in range(7))


class Tally:

    def __init__(self):
        self.n, self.i, self.per = {}, None, {}

    def value(self, sem):
        n = self.n.get(sem.name, 0)
        per = self.per.get(sem.name, 0)
        return n if self.i is None or not per else self.i * per + n

    def next(self, sem, k=1):
        self.n[sem.name] = self.n.get(sem.name, 0) + k
        return self.value(sem)

    @contextmanager
    def loop(self, eng, start, count, per):
        before = dict(self.n)
        self.per = {s.name: k for s, k in per.items()}
        if start:
            for s in self.per:
                self.n[s] = self.n.get(s, 0) - start * self.per[s]
        with eng.Fori(start, count) as i:
            self.i = i
            yield i
        if start:
            for s in self.per:
                self.n[s] += start * self.per[s]
        got = {s: self.n[s] - before.get(s, 0) for s in self.n if self.n[s] - before.get(s, 0)}
        assert got == {s: k for s, k in self.per.items() if k}, (got, self.per)
        self.i = None
        for s, k in self.per.items():
            self.n[s] = (count - start) * k + before.get(s, 0)
        self.per = {}


def build(nc, x, mem, positions, norm_g, mem_g, final_g, w_in_ab, pool_w, pool_scale, w_out_ab,
          ffn_w_gate, ffn_w_up, ffn_w_down, w_in_c, cmp_pe_k, cmp_pe_v, cmp_k_w1, cmp_k_w2,
          cmp_v_w1, cmp_v_w2, w_out_c, router_w, moe_w_gate, moe_w_up, moe_w_down,
          xa_wq, xa_wkv, xa_wo, out):
    ctx = ExitStack()
    with ctx:
        def sb(name, shape, dt=F32):
            return ctx.enter_context(nc.sbuf_tensor(name, shape, dt))

        def sem(name):
            return ctx.enter_context(nc.semaphore(name))

        ring = sb("ring", [P, RING, SLOT])
        xs = sb("xs", [P, TT, D])
        h = sb("h", [P, TT, D])
        hT = sb("hT", [P, KD, S])
        u = sb("u", [P, TT, C_IN])
        ident = sb("ident", [P, P])
        identb = sb("identb", [P, P], BF16)
        causal = sb("causal", [P, 2 * P], BF16)
        cmask = sb("cmask", [P, TT, NCMP])
        zeros = sb("zeros", [P, 2 * P])
        band = sb("band", [P, 4, TT, S])
        before = sb("before", [P, P])
        ones = sb("ones", [P, P])
        iota128 = sb("iota128", [P, P])
        iota8 = iota128[:, 0:NE]
        NROWS = 7 * KD + 2 + 2 * 16
        small = sb("small", [P, NROWS])
        gT = small[:, 0:7 * KD].rearrange("p (g k) -> p g k", g=7)
        pscale = small[:, 7 * KD:7 * KD + 2]
        pe_kv = small[:, 7 * KD + 2:NROWS].rearrange("p (v j) -> p v j", v=2)
        pw = sb("pw", [P, 2, DH])
        w2 = sb("w2", [P, 2, 2, DH])
        rw = sb("rw", [P, KD, NE])
        pos_i = sb("pos_i", [P, TT], I32)
        pos = sb("pos", [P, TT])
        eps = sb("eps", [P, 1])
        half_pi = sb("half_pi", [P, 1])
        ang = sb("ang", [P, TT, HALF])
        red = sb("red", [P, 2, TT, HALF])
        cos = sb("cos", [P, TT, HALF])
        sin = sb("sin", [P, TT, HALF])
        ss = sb("ss", [P, TT])
        rms = sb("rms", [P, TT])
        rstd = sb("rstd", [P, TT])
        kvm = sb("kvm", [P, 2, TT, 512])
        qr = sb("qr", [P, TT, 256])
        kk = sb("kk", [P, TT, 256])
        qT = sb("qT", [P, 2, S])
        kT = sb("kT", [P, 2, S])
        prob = sb("prob", [P, TT, 4, S])
        pT = sb("pT", [P, 4, 512])
        nmax = sb("nmax", [P, 8])
        rsum = sb("rsum", [P, 8])
        rinv = sb("rinv", [P, 8])
        coef = sb("coef", [P, 8])
        flat_band = band[:, :, :, :].rearrange("p a b c -> p (a b c)")
        rq = flat_band[:, 0:512].rearrange("p (t h r) -> p t h r", t=TT, h=16)
        yg = flat_band[:, 512:1024].rearrange("p (t c) -> p t c", t=TT)
        yt = flat_band[:, 1024:1536].rearrange("p (t c) -> p t c", t=TT)
        qc = yt
        qcT = yg[:, :, :]
        pooled = kT
        hid = flat_band[0:64, 1536:2048].rearrange("p (t c) -> p t c", t=2)
        moe_g, fin_g = flat_band[:, 0:D], flat_band[:, D:2 * D]
        sg = sb("sg", [P, TT, 48])
        rt = hT[:, 2:8, :].rearrange("p a b -> p (a b)").rearrange("p (j t h r) -> p j t h r", j=4, t=TT, h=24)
        kcT = sb("kcT", [P, 2 * NE])
        kcmpT = sb("kcmpT", [P, GROUPS * NCMP])
        vcmp = sb("vcmp", [16, GROUPS, DH])
        vg = sb("vg", [16, DH])
        hidT = sb("hidT", [P, 2, 2, GROUPS * NCMP])
        sc = sb("sc", [P, 8, NCMP])
        ec = sb("ec", [P, 8, NCMP])
        cmx = sb("cmx", [P, 3, 8])
        ecT = prob[0:16, 0, :, :].rearrange("p a b -> p (a b)").rearrange("p (h s) -> p h s", h=8)
        logit = sb("logit", [P, TT, NE])
        top = sb("top", [P, TT, 8])
        topi = sb("topi", [P, TT, 8], U32)
        topf = sb("topf", [P, TT, 8])
        hot = sb("hot", [P, 2, TT, NE])
        member = sb("member", [P, TT, NE])
        gap = sb("gap", [P, 4, TT])
        gate = sb("gate", [P, TT, 3 * NE])
        rank = sb("rank", [P, TT, 3 * NE])
        most = sb("most", [P, 2])
        rounds = sb("rounds", [P, 1], I32)
        mem_x = u[:, :, 0:D]
        small_rows = u[:, 0, D:D + P]
        wide = u[:, :, :].rearrange("p t c -> p (t c)")

        def area(at, *shape):
            n = math.prod(shape)
            v = wide[:, at:at + n]
            if len(shape) == 2:
                v = v.rearrange("p (a b) -> p a b", a=shape[0])
            return v

        sgate = area(0, 512)
        act = area(512, 512)
        aT = area(1024, 4, P)
        xT = area(1536, KD, P)
        outE = area(2560, D)
        sel = area(3584, TT, P)
        selg = area(3840, TT, P)
        selT = area(4096, S)
        KTp = prob[:, :, :, :].rearrange("p a b c -> p (a b) c")[:, 0:4, :]
        KT2 = pT[:, :, :].rearrange("p a b -> p (a b)").rearrange("p (v g t) -> p v g t", v=2, g=GROUPS)
        KX = hT[:, :, :].rearrange("p a b -> p (a b)")[:, 0:16 * 60].rearrange("p (j g n) -> p j g n", j=16, g=GROUPS)
        VX = hT[:, :, :].rearrange("p a b -> p (a b)")[:, 1024:1024 + 16 * 60].rearrange(
            "p (j g n) -> p j g n", j=16, g=GROUPS)

        ps = ctx.enter_context(nc.psum_tensor("ps", [P, 8, 512], F32))

        loads = [sem(f"loaded_{n}") for n in ("x", "mem", "small", "late")]
        x_loaded, mem_loaded, small_loaded, late_loaded = loads
        pool_step = sem("pool_step")
        consts_ready = sem("consts_ready")
        weights_ready = [sem(f"weights_ready_{i}") for i in range(RING)]
        weights_used = sem("weights_used")
        act_bank_full, act_bank_free = sem("act_bank_full"), sem("act_bank_free")
        scores_ready, probs_ready = sem("scores_ready"), sem("probs_ready")
        dve_bank_full, dve_bank_free = sem("dve_bank_full"), sem("dve_bank_free")
        nmax_ready = sem("nmax_ready")
        dve_step, act_step = sem("dve_step"), sem("act_step")
        x_ready, rms_ready, h_ready = sem("x_ready"), sem("rms_ready"), sem("h_ready")
        angles_ready, tables_ready = sem("angles_ready"), sem("tables_ready")
        act_staged, dve_staged = sem("act_staged"), sem("dve_staged")
        gains_loaded = sem("gains_loaded")
        rows_loaded, small_ready = sem("rows_loaded"), sem("small_ready")
        band_counted = sem("band_counted")
        counts_ready = sem("counts_ready")
        u_ready = sem("u_ready")
        heads_ready = sem("heads_ready")
        shifted = [sem(f"shifted_{i}") for i in range(8)]
        vcT_ready = sem("vcT_ready")
        cmp_in_ready = sem("cmp_in_ready")
        gates_ready = sem("gates_ready")
        cmp_shifted, cmp_exp = sem("cmp_shifted"), sem("cmp_exp")
        gate_up_full, up_full, silu_ready, act_ready = sem("gate_up_full"), sem("up_full"), sem("silu_ready"), sem("act_ready")
        turned, aT_ready = sem("turned"), sem("aT_ready")
        ffn_down_full, ffn_added = sem("ffn_down_full"), sem("ffn_added")
        down_full, down_saved = sem("down_full"), sem("down_saved")
        gap_ready, gap_exp, members_ready, routed = sem("gap_ready"), sem("gap_exp"), sem("members_ready"), sem("routed")
        sel_ready, gathered = sem("sel_ready"), sem("gathered")
        xT_low_ready, xT_high_ready = sem("xT_low_ready"), sem("xT_high_ready")
        selT_full, selT_ready = sem("selT_full"), sem("selT_ready")
        scattered, added = sem("scattered"), sem("added")
        out_ready, stored = sem("out_ready"), sem("stored")

        def cols(w, c0, n):
            return w[:, c0:c0 + n].rearrange("(k p) n -> p k n", p=P)

        def rows(w, r0, k):
            return w[bass.ds(r0, k * P), :].rearrange("(k p) n -> p k n", p=P)

        def slot_cols(slot, n):
            return ring[:, slot, :].rearrange("p (k n) -> p k n", k=KD)[:, :, 0:n]

        def slot_rows(slot, k):
            return ring[:, slot, 0:k * D].rearrange("p (k n) -> p k n", k=k)

        HEAD_UNITS = ([("c", xa_wkv[i], 0, 512) for i in range(2)]
                      + [("c", w_in_ab[0], 512 * j, 512) for j in range(5)]
                      + [("c", w_out_ab[0], 512 * j, 512) for j in range(2)]
                      + [("c", xa_wq[0], 0, 256), ("r", xa_wo[0], 0, 2)])
        IN_C = [(512 * j, min(512, C_IN - 512 * j)) for j in range(6)]
        MID_UNITS = ([("c", w_in_c[0], c0, n) for c0, n in IN_C]
                     + [("w", cmp_k_w1[0], 0, 16), ("w", cmp_v_w1[0], 0, 16)]
                     + [("c", w_out_c[0], 512 * j, 512) for j in range(2)]
                     + [("c", xa_wq[1], 0, 256), ("r", xa_wo[1], 0, 2)])
        FFN_FIRST = len(HEAD_UNITS)
        FFN_LOOP = FFN_FIRST + 1
        FFN_LAST = FFN_LOOP + 4
        MID_FIRST = FFN_LAST + 1
        MOE_FIRST = MID_FIRST + len(MID_UNITS)
        MOE_ORDER = [("g", 0), ("u", 0)]
        for s in range(1, ESTEPS):
            MOE_ORDER += [("g", s), ("u", s), ("d", s - 1)]
        MOE_ORDER += [("d", ESTEPS - 1)]
        assert len(MOE_ORDER) % RING == 0 and (FSTEPS - 1) % 2 == 0

        block = ctx.enter_context(nc.Block())

        @block.sync
        def _(sp):
            t = Tally()

            def load(slot, dsts_srcs, depth):
                slot %= RING
                n = t.value(weights_used)
                if t.i is not None or n - depth + 2 > 0:
                    if t.i is not None or n >= depth:
                        sp.wait_ge(weights_used, n - depth + 2)
                t.next(weights_used)
                for dst, src in dsts_srcs(slot):
                    sp.dma_start(dst, src).then_inc(weights_ready[slot], 16)

            def plain(unit):
                kind, w, at, n = unit
                if kind == "c":
                    return lambda s: [(slot_cols(s, n), cols(w, at, n))]
                if kind == "r":
                    return lambda s: [(slot_rows(s, n), rows(w, at, n))]
                return lambda s: [(ring[:, s, :].rearrange("p (k n) -> p k n", k=16), w.rearrange("(k p) n -> p k n", p=P))]

            def gate_up(c):
                return lambda s: [(slot_cols(s, 2 * FSTEP)[:, :, j * FSTEP:(j + 1) * FSTEP],
                                   w[0][:, bass.ds(c, FSTEP)].rearrange("(k p) n -> p k n", p=P))
                                  for j, w in enumerate((ffn_w_gate, ffn_w_up))]

            def down(r):
                return lambda s: [(slot_rows(s, 2), rows(ffn_w_down[0], r, 2))]

            sp.wait_ge(mem_loaded, 16)
            for j, unit in enumerate(HEAD_UNITS):
                load(j, plain(unit), RING)
            load(FFN_FIRST, gate_up(0), RING)
            with t.loop(sp, 0, (FSTEPS - 1) // 2, {weights_used: 4}) as i:
                for j in range(2):
                    load(FFN_LOOP + 2 * j, gate_up(i * (2 * FSTEP) + (j + 1) * FSTEP), 4)
                    load(FFN_LOOP + 2 * j + 1, down(i * (2 * FSTEP) + j * FSTEP), 4)
            load(FFN_LAST, down(FF - FSTEP), RING)
            for j, unit in enumerate(MID_UNITS):
                load(MID_FIRST + j, plain(unit), RING)

            def expert(e):
                def of(w):
                    return w[0, bass.ds(e, 1)].rearrange("e r c -> (e r) c")
                for j, (kind, s) in enumerate(MOE_ORDER):
                    if kind == "d":
                        load(MOE_FIRST + j, lambda sl: [(slot_rows(sl, 4), of(moe_w_down)[s * ESTEP:(s + 1) * ESTEP, :].rearrange(
                            "(k p) n -> p k n", p=P))], RING)
                    else:
                        w = moe_w_gate if kind == "g" else moe_w_up
                        load(MOE_FIRST + j, lambda sl: [(slot_cols(sl, ESTEP), cols(of(w), s * ESTEP, ESTEP))], RING)

            expert(0)
            sp.wait_ge(routed, 1)
            n_it = sp.value_load(rounds[0:1, 0:1], min_val=NE, max_val=2 * NE)
            with t.loop(sp, 1, n_it, {weights_used: len(MOE_ORDER)}) as it:
                expert(it % NE)
            sp.wait_ge(out_ready, 1)
            sp.dma_start(out[0].rearrange("(t p) d -> p t d", p=P), h[:, :, :]).then_inc(stored, 16)
            sp.wait_ge(stored, 16)

        @block.gpsimd
        def _(pool):
            steps = [0]

            def step(ins):
                ins.then_inc(pool_step, 1)
                steps[0] += 1
                pool.wait_ge(pool_step, steps[0])

            step(pool.memset(zeros[:, :], 0.0))
            step(pool.memset(eps[:, :], EPS))
            step(pool.memset(half_pi[:, :], math.pi / 2))
            step(pool.affine_select(out=ident[:, :], in_=zeros[:, 0:P], compare_op=ALU.not_equal, fill=1.0,
                                    base=0, pattern=[[-1, P]], channel_multiplier=1))
            pool.nop().then_inc(consts_ready, 1)
            for g, w in enumerate(WINDOWS):
                step(pool.iota(band[:, g, :, :], [[0, TT], [1, S]], base=1, channel_multiplier=0,
                               allow_small_or_imprecise_dtypes=True))
                step(pool.tensor_scalar(band[:, g, :, :], band[:, g, :, :], float(w), None, ALU.min))
            pool.nop().then_inc(band_counted, 1)
            step(pool.memset(ones[:, :], 1.0))
            step(pool.affine_select(out=identb[:, :], in_=zeros[:, 0:P], compare_op=ALU.not_equal, fill=1.0,
                                    base=0, pattern=[[-1, P]], channel_multiplier=1))
            step(pool.affine_select(out=causal[:, :], in_=zeros[:, :], compare_op=ALU.is_ge, fill=-BIG,
                                    base=P, pattern=[[-1, 2 * P]], channel_multiplier=1))
            step(pool.affine_select(out=cmask[:, :, :], in_=zeros[:, 0:TT * NCMP].rearrange("p (t n) -> p t n", t=TT),
                                    compare_op=ALU.is_ge, fill=-BIG, base=-(CMP_LEN - 1),
                                    pattern=[[P, TT], [-CMP_STRIDE, NCMP]], channel_multiplier=1))
            step(pool.affine_select(out=before[:, :], in_=zeros[:, 0:P], compare_op=ALU.is_ge, fill=1.0,
                                    base=0, pattern=[[-1, P]], channel_multiplier=1))
            step(pool.iota(iota128[:, :], [[1, P]], base=0, channel_multiplier=0, allow_small_or_imprecise_dtypes=True))
            pool.wait_ge(counts_ready, 1)
            for g, w in enumerate(WINDOWS):
                step(pool.affine_select(out=band[:, g, :, :], in_=band[:, g, :, :], compare_op=ALU.is_ge, fill=0.0,
                                        base=0, pattern=[[-P, TT], [1, S]], channel_multiplier=-1))
                step(pool.affine_select(out=band[:, g, :, :], in_=band[:, g, :, :], compare_op=ALU.is_ge, fill=0.0,
                                        base=w - 1, pattern=[[P, TT], [-1, S]], channel_multiplier=1))
            for g in range(4):
                for tt in range(TT):
                    step(pool.tensor_tensor(band[:, g, tt, tt * P:(tt + 1) * P], band[:, g, tt, tt * P:(tt + 1) * P],
                                            ident[:, :], ALU.subtract))
            pool.nop().then_inc(consts_ready, 1)
            pool.wait_ge(heads_ready, MOBA_UNITS + 1 + 1 + GROUPS + 1)
            pool.dma_start(moe_g, norm_g[1, 2].partition_broadcast(P)).then_inc(gains_loaded, 16)
            pool.dma_start(fin_g, final_g.partition_broadcast(P)).then_inc(gains_loaded, 16)

        @block.tensor
        def _(pe):
            t = Tally()
            local = {}
            first = {}
            units = [0]

            def bank(full, free, base):
                k = local.get(full.name, 0)
                local[full.name] = k + 1
                n = t.value(full)
                if k < 2:
                    need = first.get(full.name, 0)
                else:
                    need = n - 1
                if not isinstance(need, int) or need > 0:
                    pe.wait_ge(free, need)
                return base + k % 2

            def act_bank():
                return bank(act_bank_full, act_bank_free, 0)

            def score_bank():
                return bank(scores_ready, probs_ready, 2)

            def dve_bank():
                return bank(dve_bank_full, dve_bank_free, 6)

            def afresh():
                for s in (act_bank_full, scores_ready, dve_bank_full):
                    local[s.name] = 0
                    first[s.name] = t.value(s)

            def emptied():
                for full, free in ((act_bank_full, act_bank_free), (dve_bank_full, dve_bank_free)):
                    n = t.value(full)
                    if not isinstance(n, int) or n > 0:
                        pe.wait_ge(free, n)

            def unit(slot, loads=1):
                s = weights_ready[slot % RING]
                pe.wait_ge(s, t.next(s, 16 * loads))
                return slot % RING

            def project(src, slot, n, where, group=KD):
                w = slot_cols(unit(slot), n)
                for tt in range(TT):
                    full = where[tt]
                    b = act_bank() if full is act_bank_full else dve_bank()
                    for k in range(KD):
                        mm = pe.matmul(ps[:, b, 0:n], src[:, k, tt * P:(tt + 1) * P], w[:, k, :],
                                       start=(k == 0), stop=(k == KD - 1))
                        if tt == 0 and k == 0:
                            mm.then_inc(weights_used, 1)
                    mm.then_inc(full, 1)
                    t.next(full)

            def turn(blocks, full, width=P, rows_=P):
                b = act_bank() if full is act_bank_full else dve_bank()
                for j, blk in enumerate(blocks):
                    mm = pe.transpose(ps[0:width, b, j * rows_:(j + 1) * rows_], blk, ident[0:rows_, 0:rows_])
                mm.then_inc(full, 1)
                t.next(full)

            def turn_h():
                pe.wait_ge(h_ready, t.next(h_ready))
                for j in range(KD // 2):
                    turn([h[:, tt, k * P:(k + 1) * P] for k in (2 * j, 2 * j + 1) for tt in range(TT)],
                         act_bank_full if j % 2 == 0 else dve_bank_full)
                emptied()

            def turn_heads(n, full_of=lambda j: act_bank_full if j % 2 == 0 else dve_bank_full):
                pe.wait_ge(heads_ready, t.next(heads_ready))
                for j in range(n // 2):
                    turn([h[:, tt, k * P:(k + 1) * P] for k in (2 * j, 2 * j + 1) for tt in range(TT)], full_of(j))
                emptied()

            def attend(q, k_of, v_of, is_causal):
                for tt in range(TT):
                    keys = P if is_causal and tt == 0 else S
                    for par in range(2):
                        half = slice(par * DH, (par + 1) * DH)
                        b = score_bank()
                        if is_causal:
                            pe.matmul(ps[:, b, 0:2 * keys].rearrange("p (h k) -> p h k", h=2), identb[:, :],
                                      causal[:, 2 * P - keys:2 * P].unsqueeze(1).to_broadcast([P, 2, keys]),
                                      start=True, stop=False, skip_group_check=True)
                        for j in range(2):
                            mm = pe.matmul(ps[:, b, j * keys:(j + 1) * keys], q[half, j, tt * P:(tt + 1) * P],
                                           k_of(2 * j + par, half)[:, 0:keys], start=not is_causal, stop=True,
                                           skip_group_check=True)
                        mm.then_inc(scores_ready, 1)
                        t.next(scores_ready)
                blocks = [(tt, kc) for tt in range(TT) for kc in range(TT) if not is_causal or kc <= tt]
                pe.wait_ge(probs_ready, t.value(scores_ready))
                for j, (tt, kc) in enumerate(blocks):
                    turn([prob[:, tt, hd, kc * P:(kc + 1) * P] for hd in range(4)],
                         act_bank_full if j % 2 else dve_bank_full)
                emptied()
                for tt in range(TT):
                    b = dve_bank()
                    mine = [(j, kc) for j, (a, kc) in enumerate(blocks) if a == tt]
                    for hd in range(4):
                        for n, (j, kc) in enumerate(mine):
                            mm = pe.matmul(ps[:, b, hd * DH:(hd + 1) * DH], pT[:, j, hd * P:(hd + 1) * P], v_of(kc, hd),
                                           start=(n == 0), stop=(n == len(mine) - 1))
                    mm.then_inc(dve_bank_full, 1)
                    t.next(dve_bank_full)

            def pairs(stage):
                return [stage[:, tt, pr * P:(pr + 1) * P] for pr in range(2) for tt in range(TT)]

            def cross(layer, slot):
                turn_h()
                project(hT, slot, 256, (act_bank_full, dve_bank_full))
                emptied()
                turn(pairs(qr), act_bank_full)
                turn([kvm[:, layer, tt, pr * P:(pr + 1) * P] for pr in range(2) for tt in range(TT)], dve_bank_full)
                emptied()
                attend(qT, lambda hd, half: kT[half, hd // 2, :],
                       lambda kc, hd: kvm[:, layer, kc, 256 + hd * DH:256 + (hd + 1) * DH], False)
                turn_heads(2)
                w = slot_rows(unit(slot + 1), 2)
                for tt in range(TT):
                    for c in range(2):
                        b = dve_bank()
                        for k in range(2):
                            mm = pe.matmul(ps[:, b, :], hT[:, k, tt * P:(tt + 1) * P], w[:, k, c * 512:(c + 1) * 512],
                                           start=(k == 0), stop=(k == 1))
                            if tt == c == k == 0:
                                mm.then_inc(weights_used, 1)
                        mm.then_inc(dve_bank_full, 1)
                        t.next(dve_bank_full)

            pe.wait_ge(consts_ready, 1)
            pe.wait_ge(rows_loaded, 16 * 5)
            turn([small_rows[0:NROWS, :]], dve_bank_full, P, NROWS)
            turn_h()
            for layer in range(2):
                project(hT, layer, 512, (act_bank_full, dve_bank_full))
            turn_h()
            for j in range(5):
                project(hT, 2 + j, 512, (act_bank_full, dve_bank_full))
            emptied()
            pe.wait_ge(consts_ready, 2)
            pe.wait_ge(small_loaded, t.next(small_loaded, 16 * 4))
            for pr in range(2):
                b = dve_bank()
                for g in (2 * pr, 2 * pr + 1):
                    at = (g % 2) * DH
                    for st in range(TT):
                        mm = pe.matmul(ps[at:at + DH, b, 0:S], u[:, st, g * DH:(g + 1) * DH], band[:, g, st, :],
                                       start=(st == 0), stop=(st == TT - 1))
                mm.then_inc(dve_bank_full, 1)
                t.next(dve_bank_full)
            emptied()
            for pr in range(2):
                b = dve_bank()
                for j in range(2):
                    half = slice(j * DH, (j + 1) * DH)
                    mm = pe.matmul(ps[half, b, 0:S], pw[half, pr, :], pooled[half, pr, :], start=True, stop=True)
                mm.then_inc(dve_bank_full, 1)
                t.next(dve_bank_full)
            afresh()
            with t.loop(pe, 0, MOBA_UNITS, {act_staged: 1, dve_staged: 1, act_bank_full: 2, dve_bank_full: 5,
                                            scores_ready: 4, heads_ready: 1}) as i:
                t.next(heads_ready)
                first.update({s.name: t.value(s) for s in (act_bank_full, scores_ready, dve_bank_full)})
                pe.wait_ge(act_staged, t.next(act_staged))
                pe.wait_ge(dve_staged, t.next(dve_staged))
                turn(pairs(qr), act_bank_full)
                turn(pairs(kk), dve_bank_full)
                emptied()
                attend(qT, lambda hd, half: kT[half, hd // 2, :],
                       lambda kc, hd: u[:, kc, bass.ds(i * 256 + (POOL + 2 * MOBA + hd * DH), DH)], True)
            afresh()
            turn_heads(MOBA // P)
            for j in range(2):
                project(hT, 7 + j, 512, (dve_bank_full, dve_bank_full))
            cross(0, 9)

            turn_h()

            def gate_up(w, tt, signal_unit):
                n = t.value(gate_up_full) - (TT - 1)
                if t.i is not None or n > 0:
                    pe.wait_ge(act_ready, n)
                for k in range(KD):
                    mm = pe.matmul(ps[:, 4 + tt, :], hT[:, k, tt * P:(tt + 1) * P], w[:, k, :],
                                   start=(k == 0), stop=(k == KD - 1))
                    if signal_unit and k == 0:
                        mm.then_inc(weights_used, 1)
                mm.then_inc(gate_up_full, 1)
                t.next(gate_up_full)

            def turn_act():
                pe.wait_ge(act_ready, t.value(gate_up_full) - turn_act.behind)
                for kc in range(2):
                    for tt in range(TT):
                        mm = pe.transpose(ps[:, 6, (kc * TT + tt) * P:(kc * TT + tt + 1) * P],
                                          act[:, tt * FSTEP + kc * P:tt * FSTEP + (kc + 1) * P], ident[:, :])
                mm.then_inc(turned, 1)
                t.next(turned)

            def down(slot, start, stop):
                w = slot_rows(unit(slot), 2)
                pe.wait_ge(aT_ready, t.value(turned))
                for tt in range(TT):
                    for c in range(2):
                        for kc in range(2):
                            mm = pe.matmul(ps[:, 2 * tt + c, :], aT[:, kc * TT + tt, :], w[:, kc, c * 512:(c + 1) * 512],
                                           start=(start and kc == 0), stop=(stop and kc == 1), skip_group_check=True)
                            if tt == c == kc == 0:
                                mm.then_inc(weights_used, 1)
                return mm

            pe.wait_ge(probs_ready, t.value(scores_ready))
            w = slot_cols(unit(FFN_FIRST, 2), 512)
            for tt in range(TT):
                gate_up(w, tt, tt == 0)
            for b in range(4):
                pe.matmul(ps[:, b, :], zeros[:, 0:P], slot_cols((FFN_FIRST) % RING, 512)[:, 0, :], start=True, stop=False,
                          skip_group_check=True)
            per = {weights_ready[(FFN_LOOP + j) % RING]: (32, 16)[j % 2] for j in range(4)}
            with t.loop(pe, 0, (FSTEPS - 1) // 2, {**per, gate_up_full: 4, turned: 2}) as i:
                for j in range(2):
                    w = slot_cols(unit(FFN_LOOP + 2 * j, 2), 512)
                    gate_up(w, 0, True)
                    turn_act.behind = 1
                    turn_act()
                    gate_up(w, 1, False)
                    down(FFN_LOOP + 2 * j + 1, False, False)
            turn_act.behind = 0
            turn_act()
            down(FFN_LAST, False, True).then_inc(ffn_down_full, 1)
            pe.wait_ge(ffn_added, 1)

            turn_h()
            for j, (c0, n) in enumerate(IN_C):
                project(hT, MID_FIRST + j, n, (act_bank_full, dve_bank_full))
            emptied()
            for c0 in (KC0, VC0):
                turn([u[:, tt, c0 + pr * P:c0 + (pr + 1) * P] for pr in range(2) for tt in range(TT)],
                     act_bank_full if c0 == KC0 else dve_bank_full)
            pe.wait_ge(cmp_in_ready, t.next(cmp_in_ready))
            for v, X in enumerate((KX, VX)):
                s = unit(MID_FIRST + len(IN_C) + v)
                w = ring[:, s, :].rearrange("p (k n) -> p k n", k=16)
                b = act_bank()
                for j in range(16):
                    mm = pe.matmul(ps[0:GROUPS * NCMP, b, 0:CMP_HID], X[:, j].rearrange("p g n -> p (g n)"), w[:, j, :],
                                   start=(j == 0), stop=(j == 15))
                    if j == 0:
                        mm.then_inc(weights_used, 1)
                mm.then_inc(act_bank_full, 1)
                t.next(act_bank_full)
            emptied()
            turn([hid[0:GROUPS * NCMP, v, kc * P:(kc + 1) * P] for v in range(2) for kc in range(2)],
                 dve_bank_full, P, GROUPS * NCMP)
            emptied()
            b = dve_bank()
            for at in (0, DH):
                for kc in range(2):
                    mm = pe.matmul(ps[at:at + DH, b, 0:GROUPS * NCMP], w2[:, 0, kc, :], hidT[:, 0, kc, :],
                                   start=(kc == 0), stop=(kc == 1))
            mm.then_inc(dve_bank_full, 1)
            t.next(dve_bank_full)
            b = dve_bank()
            for g in range(GROUPS):
                for kc in range(2):
                    mm = pe.matmul(ps[0:NCMP, b, g * DH:(g + 1) * DH], hidT[:, 1, kc, g * NCMP:(g + 1) * NCMP],
                                   w2[:, 1, kc, :], start=(kc == 0), stop=(kc == 1))
            mm.then_inc(dve_bank_full, 1)
            t.next(dve_bank_full)
            afresh()
            with t.loop(pe, 0, GROUPS, {act_staged: 1, dve_staged: 1, act_bank_full: 4, dve_bank_full: 15,
                                        scores_ready: 8, cmp_exp: 1, heads_ready: 1}) as g:
                t.next(heads_ready)
                first.update({s.name: t.value(s) for s in (act_bank_full, scores_ready, dve_bank_full)})
                pe.wait_ge(act_staged, t.next(act_staged))
                pe.wait_ge(dve_staged, t.next(dve_staged))
                turn(pairs(qr), act_bank_full)
                turn(pairs(kk), dve_bank_full)
                turn(pairs(qc), act_bank_full)
                emptied()
                for par in range(2):
                    b = dve_bank()
                    half = slice(par * DH, (par + 1) * DH)
                    for tt in range(TT):
                        for j in range(2):
                            c = (tt * 2 + j) * 16
                            mm = pe.matmul(ps[:, b, c:c + NCMP], qcT[half, j, tt * P:(tt + 1) * P], kcT[half, 0:NCMP],
                                           start=True, stop=True)
                    mm.then_inc(dve_bank_full, 1)
                    t.next(dve_bank_full)
                for which, v0 in enumerate((VS0, VW0)):
                    attend(qT, lambda hd, half: kT[half, which, :],
                           lambda kc, hd: u[:, kc, bass.ds(g * DH + v0, DH)], True)
                pe.wait_ge(cmp_exp, t.next(cmp_exp))
                for tt in range(TT):
                    b = dve_bank()
                    for hd in range(4):
                        mm = pe.transpose(ps[0:NCMP, b, hd * P:(hd + 1) * P], ec[:, tt * 4 + hd, :], ident[:, :])
                    mm.then_inc(dve_bank_full, 1)
                    t.next(dve_bank_full)
                emptied()
                for tt in range(TT):
                    b = dve_bank()
                    for hd in range(4):
                        mm = pe.matmul(ps[:, b, hd * DH:(hd + 1) * DH], ecT[0:NCMP, tt * 4 + hd, :],
                                       vg[0:NCMP, :], start=True, stop=True)
                    mm.then_inc(dve_bank_full, 1)
                    t.next(dve_bank_full)
            afresh()
            turn_heads(KD)
            for j in range(2):
                project(hT, MOE_FIRST - 4 + j, 512, (dve_bank_full, dve_bank_full))
            cross(1, MOE_FIRST - 2)

            turn_h()
            b = dve_bank()
            for tt in range(TT):
                for k in range(KD):
                    mm = pe.matmul(ps[:, b, tt * NE:(tt + 1) * NE], hT[:, k, tt * P:(tt + 1) * P], rw[:, k, :],
                                   start=(k == 0), stop=(k == KD - 1))
            mm.then_inc(dve_bank_full, 1)
            t.next(dve_bank_full)
            pe.wait_ge(members_ready, t.next(members_ready))
            b = dve_bank()
            pe.matmul(ps[:, b, 0:NE], before[:, :], member[:, 0, :], start=True, stop=True)
            pe.matmul(ps[:, b, NE:2 * NE], ones[:, :], member[:, 0, :], start=True, stop=False)
            pe.matmul(ps[:, b, NE:2 * NE], before[:, :], member[:, 1, :], start=False, stop=True)
            pe.matmul(ps[:, b, 2 * NE:3 * NE], ones[:, :], member[:, 0, :], start=True, stop=False)
            pe.matmul(ps[:, b, 2 * NE:3 * NE], ones[:, :], member[:, 1, :], start=False, stop=True).then_inc(dve_bank_full, 1)
            t.next(dve_bank_full)
            emptied()
            pe.wait_ge(probs_ready, t.value(scores_ready))

            def gather():
                pe.wait_ge(sel_ready, t.next(sel_ready))
                for k in range(KD):
                    for tt in range(TT):
                        mm = pe.matmul(ps[:, 2 + k // 4, (k % 4) * P:(k % 4 + 1) * P], h[:, tt, k * P:(k + 1) * P],
                                       sel[:, tt, :], start=(tt == 0), stop=(tt == TT - 1))
                mm.then_inc(gathered, 1)
                t.next(gathered)

            def scatter():
                pe.wait_ge(down_saved, t.value(down_full) + 1)
                pe.wait_ge(selT_ready, t.value(selT_full) + 1)
                for tt in range(TT):
                    for c in range(2):
                        mm = pe.matmul(ps[:, (2, 3, 6, 7)[2 * tt + c], :], selT[:, tt * P:(tt + 1) * P],
                                       outE[:, c * 512:(c + 1) * 512], start=True, stop=True)
                mm.then_inc(scattered, 1)
                t.next(scattered)

            def moe_wide(slot, bnk, full):
                w = slot_cols(unit(slot), ESTEP)
                for k in range(KD):
                    mm = pe.matmul(ps[:, bnk, :], xT[:, k, :], w[:, k, :], start=(k == 0), stop=(k == KD - 1))
                    if k == 0:
                        mm.then_inc(weights_used, 1)
                mm.then_inc(full, 1)
                t.next(full)

            def moe_turn():
                pe.wait_ge(act_ready, t.next(act_ready))
                for kc in range(4):
                    mm = pe.transpose(ps[:, 6, kc * P:(kc + 1) * P], act[:, kc * P:(kc + 1) * P], ident[:, :])
                mm.then_inc(turned, 1)
                t.next(turned)

            def moe_down(slot, start, stop):
                w = slot_rows(unit(slot), 4)
                pe.wait_ge(aT_ready, t.value(turned))
                for c in range(2):
                    for kc in range(4):
                        mm = pe.matmul(ps[:, c, :], aT[:, kc, :], w[:, kc, c * 512:(c + 1) * 512],
                                       start=(start and kc == 0), stop=(stop and kc == 3), skip_group_check=True)
                        if c == kc == 0:
                            mm.then_inc(weights_used, 1)
                return mm

            t.n[act_ready.name] = t.n[gate_up_full.name]
            pe.wait_ge(routed, 1)
            n_it = pe.value_load(rounds[0:1, 0:1], min_val=NE, max_val=2 * NE)
            gather()
            per = {w: 48 for w in weights_ready}
            with t.loop(pe, 0, n_it, {**per, gate_up_full: ESTEPS, up_full: ESTEPS, turned: ESTEPS, act_ready: ESTEPS,
                                      sel_ready: 1, gathered: 1, scattered: 1, added: 1, selT_full: 1,
                                      down_full: 1}) as it:
                slots = {ks: MOE_FIRST + j for j, ks in enumerate(MOE_ORDER)}
                pe.wait_ge(xT_low_ready, t.value(gathered))
                pe.wait_ge(xT_high_ready, t.value(gathered))
                for s in range(ESTEPS):
                    moe_wide(slots["g", s], 4, gate_up_full)
                    moe_wide(slots["u", s], 5, up_full)
                    if s == 0:
                        scatter()
                        pe.wait_ge(added, t.next(added))
                    else:
                        moe_down(slots["d", s - 1], s == 1, False)
                    if s < ESTEPS - 1:
                        moe_turn()
                pe.wait_ge(act_ready, t.value(gate_up_full))
                for tt in range(TT):
                    mm = pe.transpose(ps[:, 7, tt * P:(tt + 1) * P], selg[:, tt, :], ident[:, :])
                mm.then_inc(selT_full, 1)
                t.next(selT_full)
                moe_turn()
                gather()
                moe_down(slots["d", ESTEPS - 1], False, True).then_inc(down_full, 1)
                t.next(down_full)
            pe.wait_ge(xT_low_ready, t.value(gathered))
            pe.wait_ge(xT_high_ready, t.value(gathered))
            scatter()

        @block.scalar
        def _(sc_):
            t = Tally()

            def step(ins):
                ins.then_inc(act_step, 1)
                sc_.wait_ge(act_step, t.next(act_step))

            def bank():
                k = bank.k
                bank.k += 1
                sc_.wait_ge(act_bank_full, t.next(act_bank_full))
                return k % 2
            bank.k = 0

            def freed(ins):
                ins.then_inc(act_bank_free, 1)
                t.next(act_bank_free)

            def own_evacs():
                sc_.wait_ge(act_bank_free, t.value(act_bank_free))

            def norm():
                sc_.wait_ge(x_ready, t.next(x_ready))
                for tt in range(TT):
                    ins = sc_.activation(h[:, tt, :], (mem_x if norm.mem else xs)[:, tt, :], ACT.Square, accum_out=ss[:, tt:tt + 1])
                step(ins)
                sc_.activation(rms[:, :], ss[:, :], ACT.Sqrt, scale=1.0 / D, bias=eps[:, 0:1]).then_inc(rms_ready, 1)
            norm.mem = False

            def turn_h(gain):
                for j in (0, 2):
                    b = bank()
                    for n in range(2):
                        ins = sc_.activation(hT[:, 2 * j + n, :], ps[:, b, n * S:(n + 1) * S], ACT.Copy,
                                             scale=gT[:, gain, 2 * j + n:2 * j + n + 1])
                    freed(ins)

            def turn_heads(at, n):
                for j in range(0, n // 2, 2):
                    b = bank()
                    freed(sc_.activation(hT[:, at + 2 * j:at + 2 * j + 2, :].rearrange("p k s -> p (k s)"), ps[:, b, :], ACT.Copy))

            def save(dst, n):
                b = bank()
                freed(sc_.activation(dst, ps[:, b, 0:n], ACT.Copy))

            def attend(is_causal):
                for tt in range(TT):
                    keys = P if is_causal and tt == 0 else S
                    for par in range(2):
                        sc_.wait_ge(nmax_ready, t.next(nmax_ready))
                        for j in range(2):
                            hd = 2 * j + par
                            c = tt * 4 + hd
                            ins = sc_.activation(prob[:, tt, hd, 0:keys], ps[:, 2 + par, j * keys:(j + 1) * keys], ACT.Exp,
                                                 bias=nmax[:, c:c + 1], accum_out=rsum[:, c:c + 1])
                        ins.then_inc(probs_ready, 1)
                for j in range(3 if is_causal else 4):
                    if j % 2:
                        b = bank()
                        freed(sc_.activation(pT[:, j, :], ps[:, b, :], ACT.Copy))

            def afresh():
                bank.k = 0

            def cross(layer):
                norm()
                turn_h(3 * layer + 1)
                save(qr[:, 0, :], 256)
                b = bank()
                freed(sc_.activation(qT[:, :, :].rearrange("p a s -> p (a s)"), ps[:, b, :], ACT.Copy, scale=SCALE))
                attend(False)
                turn_heads(0, 2)

            sc_.dma_start(mem_x, mem[0].rearrange("(t p) d -> p t d", p=P)).then_inc(mem_loaded, 16)
            rows_at = 0
            for src in (norm_g.rearrange("l n (k p) -> (l n k) p", p=P), mem_g.rearrange("(k p) -> k p", p=P),
                        pool_scale[0].rearrange("(k p) -> k p", p=P),
                        cmp_pe_k[0].rearrange("(j r) d -> j (r d)", r=2), cmp_pe_v[0].rearrange("(j r) d -> j (r d)", r=2)):
                sc_.dma_start(small_rows[rows_at:rows_at + src.shape[0], :], src).then_inc(rows_loaded, 16)
                rows_at += src.shape[0]
            assert rows_at == NROWS
            sc_.dma_start(xs[:, :, :], x[0].rearrange("(t p) d -> p t d", p=P)).then_inc(x_loaded, 16)
            with nc.allow_non_contiguous_dma(reason="small"):
                sc_.dma_start(pos_i[:, :], positions.rearrange("(t p) -> p t", p=P)).then_inc(small_loaded, 16)
                for j in range(2):
                    sc_.dma_start(pw[j * DH:(j + 1) * DH, :, :],
                                  pool_w[0].rearrange("(r j) c d -> j c r d", j=2)[j]).then_inc(small_loaded, 16)
                sc_.dma_start(rw[:, :, :], router_w[0].rearrange("(k p) e -> p k e", p=P)).then_inc(small_loaded, 16)
                for v, w_ in enumerate((cmp_k_w2, cmp_v_w2)):
                    sc_.dma_start(w2[:, v, :, :], w_[0].rearrange("(k p) d -> p k d", p=P)).then_inc(late_loaded, 16)

            norm.mem = True
            sc_.wait_ge(mem_loaded, 16)
            sc_.wait_ge(consts_ready, 1)
            norm()
            norm.mem = False
            sc_.wait_ge(small_ready, 1)
            turn_h(6)
            for layer in range(2):
                save(kvm[:, layer, 0, :], 512)
            sc_.wait_ge(x_loaded, 16)
            norm()
            turn_h(0)
            for j in range(5):
                save(u[:, 0, 512 * j:512 * (j + 1)], 512)
            sc_.wait_ge(angles_ready, t.next(angles_ready))
            sc_.activation(sin[:, :, :], red[:, 0], ACT.Sin).then_inc(tables_ready, 1)
            sc_.activation(cos[:, :, :], red[:, 1], ACT.Sin, scale=-1.0, bias=half_pi[:, 0:1]).then_inc(tables_ready, 1)
            sc_.wait_ge(u_ready, t.next(u_ready))
            afresh()
            with t.loop(sc_, 0, MOBA_UNITS, {act_bank_full: 2, act_bank_free: 2, nmax_ready: 4, heads_ready: 1}) as i:
                sc_.activation(qr[:, :, :], u[:, :, bass.ds(i * 256 + POOL, 256)], ACT.Copy).then_inc(act_staged, 1)
                b = bank()
                freed(sc_.activation(qT[:, :, :].rearrange("p a s -> p (a s)"), ps[:, b, :], ACT.Copy, scale=SCALE))
                attend(True)
                sc_.wait_ge(heads_ready, t.next(heads_ready))
            afresh()
            turn_heads(2, MOBA // P)
            t.next(heads_ready)
            cross(0)
            t.next(heads_ready)
            norm()
            turn_h(2)

            def silu(tt):
                sc_.wait_ge(gate_up_full, t.next(gate_up_full))
                sc_.activation(sgate[:, tt * FSTEP:(tt + 1) * FSTEP], ps[:, 4 + tt, 0:FSTEP], ACT.Silu).then_inc(silu_ready, 1)

            def save_turned():
                sc_.wait_ge(turned, t.next(turned))
                sc_.activation(aT[:, :, :].rearrange("p a b -> p (a b)"), ps[:, 6, :], ACT.Copy).then_inc(aT_ready, 1)

            silu(0)
            silu(1)
            with t.loop(sc_, 0, (FSTEPS - 1) // 2, {gate_up_full: 4, turned: 2}) as i:
                for j in range(2):
                    silu(0)
                    save_turned()
                    silu(1)
            save_turned()
            norm()
            turn_h(3)
            for j, (c0, n) in enumerate(IN_C):
                save(u[:, 0, c0:c0 + n], n)
            sc_.wait_ge(u_ready, t.next(u_ready))
            own_evacs()
            sc_.activation(sg[:, :, :], u[:, :, GL0:GL0 + 48], ACT.Sigmoid).then_inc(gates_ready, 1)
            b = bank()
            freed(sc_.activation(KTp[:, 0:2, :].rearrange("p a b -> p (a b)"), ps[:, b, :], ACT.Copy))
            own_evacs()
            for v in range(2):
                if v == 1:
                    sc_.wait_ge(vcT_ready, 1)
                for par in range(2):
                    src = KTp[par * DH:(par + 1) * DH, 2 * v:2 * v + 2, :]
                    sc_.dma_start(KT2[0:DH, v, par:GROUPS:2, :], src).then_inc(shifted[4 * v + 2 * par], 16)
                    sc_.dma_start(KT2[DH:P, v, par:GROUPS:2, 0:S - 1], src[:, :, 1:S]).then_inc(shifted[4 * v + 2 * par + 1], 16)
            for v in range(2):
                b = bank()
                freed(sc_.activation(hid[0:GROUPS * NCMP, v, :], ps[0:GROUPS * NCMP, b, 0:CMP_HID], ACT.Gelu_apprx_tanh))
            afresh()
            with t.loop(sc_, 0, GROUPS, {act_bank_full: 4, act_bank_free: 4, nmax_ready: 8, heads_ready: 1, cmp_shifted: 1}) as g:
                sc_.activation(qc[:, :, :], u[:, :, bass.ds(g * 256, 256)], ACT.Copy)
                for tt in range(TT):
                    ins = sc_.activation(qr[:, tt, :].rearrange("p (h d) -> p h d", h=4)[:, :, ROPE:DH],
                                         u[:, tt, bass.ds(g * 256, 256)].rearrange("p (h d) -> p h d", h=4)[:, :, ROPE:DH],
                                         ACT.Copy)
                ins.then_inc(act_staged, 1)
                for dst in (qT, qcT):
                    b = bank()
                    freed(sc_.activation(dst[:, :, :].rearrange("p a s -> p (a s)"), ps[:, b, :], ACT.Copy, scale=SCALE))
                sc_.wait_ge(cmp_shifted, t.next(cmp_shifted))
                sc_.activation(ec[:, :, :], sc[:, :, :], ACT.Exp).then_inc(cmp_exp, 1)
                attend(True)
                attend(True)
                sc_.wait_ge(heads_ready, t.next(heads_ready))
            afresh()
            turn_heads(0, KD)
            t.next(heads_ready)
            cross(1)
            norm()
            turn_h(5)
            sc_.wait_ge(gap_ready, t.next(gap_ready))
            sc_.activation(gap[:, 1, :], gap[:, 0, :], ACT.Exp).then_inc(gap_exp, 1)
            sc_.wait_ge(routed, 1)
            n_it = sc_.value_load(rounds[0:1, 0:1], min_val=NE, max_val=2 * NE)

            def save_x():
                sc_.wait_ge(gathered, t.next(gathered))
                sc_.activation(xT[:, 0:4, :].rearrange("p a b -> p (a b)"), ps[:, 2, :], ACT.Copy).then_inc(xT_low_ready, 1)

            save_x()
            sc_.activation(outE[:, :].rearrange("p (c n) -> p c n", c=4), zeros[:, :].unsqueeze(1).to_broadcast([P, 4, 2 * P]),
                           ACT.Copy).then_inc(down_saved, 1)
            sc_.activation(selT[:, :], zeros[:, :], ACT.Copy).then_inc(selT_ready, 1)
            with t.loop(sc_, 0, n_it, {gate_up_full: ESTEPS, turned: ESTEPS, selT_full: 1, gathered: 1, down_full: 1}) as it:
                for s in range(ESTEPS):
                    sc_.wait_ge(gate_up_full, t.next(gate_up_full))
                    sc_.activation(sgate[:, :], ps[:, 4, :], ACT.Silu).then_inc(silu_ready, 1)
                    if s < ESTEPS - 1:
                        save_turned()
                sc_.wait_ge(selT_full, t.next(selT_full))
                sc_.activation(selT[:, :], ps[:, 7, 0:S], ACT.Copy).then_inc(selT_ready, 1)
                save_turned()
                save_x()
                sc_.wait_ge(down_full, t.next(down_full))
                sc_.activation(outE[:, :].rearrange("p (c n) -> p c n", c=2), ps[:, 0:2, :], ACT.Copy).then_inc(down_saved, 1)
            norm()

        @block.vector
        def _(ve):
            t = Tally()

            def step(ins):
                ins.then_inc(dve_step, 1)
                ve.wait_ge(dve_step, t.next(dve_step))

            def bank():
                k = bank.k
                bank.k += 1
                ve.wait_ge(dve_bank_full, t.next(dve_bank_full))
                return 6 + k % 2
            bank.k = 0

            def freed(ins):
                ins.then_inc(dve_bank_free, 1)
                t.next(dve_bank_free)

            def own_evacs():
                ve.wait_ge(dve_bank_free, t.value(dve_bank_free))

            def norm(src):
                ve.wait_ge(rms_ready, t.next(rms_ready))
                step(ve.reciprocal(rstd[:, :], rms[:, :]))
                for tt in range(TT):
                    ins = ve.tensor_scalar(h[:, tt, :], src[:, tt, :], rstd[:, tt:tt + 1], None, ALU.mult)
                ins.then_inc(h_ready, 1)
                t.next(h_ready)

            def x_stands():
                own_evacs()
                ve.nop().then_inc(x_ready, 1)

            def turn_h(gain):
                for j in (1, 3):
                    b = bank()
                    for n in range(2):
                        ins = ve.tensor_scalar(hT[:, 2 * j + n, :], ps[:, b, n * S:(n + 1) * S],
                                               gT[:, gain, 2 * j + n:2 * j + n + 1], None, ALU.mult)
                    freed(ins)

            def turn_heads(at, n):
                for j in range(1, n // 2, 2):
                    b = bank()
                    freed(ve.tensor_copy(hT[:, at + 2 * j:at + 2 * j + 2, :].rearrange("p k s -> p (k s)"), ps[:, b, :]))

            def save(dst, n):
                b = bank()
                freed(ve.tensor_copy(dst, ps[:, b, 0:n]))

            def add_x(tt, c):
                b = bank()
                part = xs[:, tt, c * 512:(c + 1) * 512]
                freed(ve.tensor_tensor(part, ps[:, b, :], part, ALU.add))

            def heads_stand():
                own_evacs()
                ve.nop().then_inc(heads_ready, 1)

            def attend(is_causal, result):
                for tt in range(TT):
                    keys = P if is_causal and tt == 0 else S
                    for par in range(2):
                        ve.wait_ge(scores_ready, t.next(scores_ready))
                        ve.tensor_reduce(nmax[:, 4 * tt + par:4 * tt + 4:2],
                                         ps[:, 2 + par, 0:2 * keys].rearrange("p (h k) -> p h k", h=2), AX, ALU.max,
                                         negate=True).then_inc(nmax_ready, 1)
                for j in range(3 if is_causal else 4):
                    if j % 2 == 0:
                        b = bank()
                        freed(ve.tensor_copy(pT[:, j, :], ps[:, b, :]))
                for tt in range(TT):
                    b = bank()
                    if tt == 0:
                        step(ve.reciprocal(rinv[:, :], rsum[:, :]))
                    result(tt, b)

            def afresh():
                bank.k = 0

            def per_head(v, n=4):
                return v.rearrange("p (h d) -> p h d", h=n)

            def wide_of(c, n):
                return c.unsqueeze(2).to_broadcast([P, n, DH])

            def rotate(lo, hi, out_lo, out_hi, n):
                c = cos[:, :, :].unsqueeze(2).to_broadcast([P, TT, n, HALF])
                s = sin[:, :, :].unsqueeze(2).to_broadcast([P, TT, n, HALF])
                r = [rt[:, j, :, 0:n, :] for j in range(4)]
                ve.tensor_tensor(r[0], lo, c, ALU.mult)
                ve.tensor_tensor(r[1], hi, s, ALU.mult)
                ve.tensor_tensor(r[2], lo, s, ALU.mult)
                step(ve.tensor_tensor(r[3], hi, c, ALU.mult))
                ve.tensor_tensor(out_lo, r[0], r[1], ALU.subtract)
                step(ve.tensor_tensor(out_hi, r[2], r[3], ALU.add))

            def cross(layer):
                norm(xs)
                turn_h(3 * layer + 1)
                save(qr[:, 1, :], 256)
                save(kT[:, :, :].rearrange("p a s -> p (a s)"), 512)

                def result(tt, b):
                    freed(ve.tensor_tensor(per_head(h[:, tt, 0:256]), per_head(ps[:, b, 0:256]),
                                           wide_of(rinv[:, 4 * tt:4 * tt + 4], 4), ALU.mult))
                attend(False, result)
                heads_stand()
                turn_heads(0, 2)
                for tt in range(TT):
                    for c in range(2):
                        add_x(tt, c)
                x_stands()

            ve.wait_ge(mem_loaded, 16)
            ve.nop().then_inc(x_ready, 1)
            norm(mem_x)
            b = bank()
            ve.tensor_copy(small[:, :], ps[:, b, 0:NROWS]).then_inc(small_ready, 1)
            ve.wait_ge(small_ready, 1)
            freed(ve.nop())
            turn_h(6)
            for layer in range(2):
                save(kvm[:, layer, 1, :], 512)
            own_evacs()
            ve.wait_ge(x_loaded, 16)
            ve.nop().then_inc(x_ready, 1)
            norm(xs)
            turn_h(0)
            ve.wait_ge(small_loaded, 16 * 4)
            step(ve.tensor_copy(pos[:, :], pos_i[:, :]))
            for j in range(HALF):
                inv = float(np.float32(np.float32(THETA) ** np.float32(-2.0 * j / ROPE)))
                ins = ve.tensor_scalar(ang[:, :, j], pos[:, :], inv, None, ALU.mult)
            step(ins)
            step(ve.tensor_scalar(red[:, 1], ang[:, :, :], 1.0 / (2 * math.pi), MAGIC, ALU.mult, ALU.add))
            step(ve.tensor_scalar(red[:, 1], red[:, 1], MAGIC, None, ALU.subtract))
            prev = ang[:, :, :]
            for part in (*TWO_PI, TWO_PI_REST):
                step(ve.scalar_tensor_tensor(red[:, 0], red[:, 1], -part, prev, ALU.mult, ALU.add))
                prev = red[:, 0]
            step(ve.tensor_scalar(red[:, 0], red[:, 0], math.pi - 1e-6, -(math.pi - 1e-6), ALU.min, ALU.max))
            step(ve.tensor_scalar(red[:, 1], red[:, 0], -1.0, None, ALU.mult))
            ve.tensor_tensor(red[:, 1], red[:, 1], red[:, 0], ALU.max).then_inc(angles_ready, 1)
            ve.wait_ge(band_counted, 1)
            for j in range(5):
                save(u[:, 1, 512 * j:512 * (j + 1)], 512)
                if j < 4:
                    ins = ve.reciprocal(band[:, j, :, :], band[:, j, :, :])
                    if j == 3:
                        ins.then_inc(counts_ready, 1)
            own_evacs()
            ve.wait_ge(consts_ready, 2)
            ve.wait_ge(late_loaded, 16 * 2)
            ve.wait_ge(act_bank_free, 2 + 2 + 2 + 5)
            for pr in range(2):
                save(pooled[:, pr, :], S)
            for pr in range(2):
                b = bank()
                freed(ve.tensor_scalar(hT[:, pr, :], ps[:, b, 0:S], pscale[:, pr:pr + 1], None, ALU.mult))
            ve.wait_ge(tables_ready, 2)
            qk = u[:, :, POOL:POOL + 2 * MOBA].rearrange("p t (h d) -> p t h d", d=DH)
            rotate(qk[:, :, :, 0:HALF], qk[:, :, :, HALF:ROPE], qk[:, :, :, 0:HALF], qk[:, :, :, HALF:ROPE], 2 * MOBA // DH)
            ve.nop().then_inc(u_ready, 1)
            afresh()
            with t.loop(ve, 0, MOBA_UNITS, {dve_bank_full: 5, dve_bank_free: 5, dve_step: 1, scores_ready: 4}) as i:
                ve.tensor_copy(kk[:, :, :], u[:, :, bass.ds(i * 256 + (POOL + MOBA), 256)]).then_inc(dve_staged, 1)
                save(kT[:, :, :].rearrange("p a s -> p (a s)"), 512)

                def result(tt, b):
                    freed(ve.tensor_tensor(per_head(h[:, tt, bass.ds(i * 256, 256)]), per_head(ps[:, b, 0:256]),
                                           wide_of(rinv[:, 4 * tt:4 * tt + 4], 4), ALU.mult))
                attend(True, result)
                heads_stand()
            afresh()
            heads_stand()
            turn_heads(2, MOBA // P)
            for c in range(2):
                for tt in range(TT):
                    add_x(tt, c)
            x_stands()
            cross(0)
            norm(xs)
            turn_h(2)

            def times_up(tt):
                ve.wait_ge(silu_ready, t.next(silu_ready))
                part = slice(tt * FSTEP, (tt + 1) * FSTEP)
                ve.tensor_tensor(act[:, part], ps[:, 4 + tt, FSTEP:2 * FSTEP], sgate[:, part], ALU.mult).then_inc(act_ready, 1)

            times_up(0)
            times_up(1)
            with t.loop(ve, 0, (FSTEPS - 1) // 2, {silu_ready: 4, turned: 2}) as i:
                for j in range(2):
                    ve.wait_ge(turned, t.next(turned))
                    times_up(0)
                    times_up(1)
            ve.wait_ge(ffn_down_full, 1)
            for tt in range(TT):
                part = xs[:, tt, :].rearrange("p (c n) -> p c n", c=2)
                ins = ve.tensor_tensor(part, ps[:, 2 * tt:2 * tt + 2, :], part, ALU.add)
            ins.then_inc(ffn_added, 1)
            ve.wait_ge(ffn_added, 1)
            ve.nop().then_inc(x_ready, 1)
            norm(xs)
            turn_h(3)
            for j, (c0, n) in enumerate(IN_C):
                save(u[:, 1, c0:c0 + n], n)
            own_evacs()
            ve.nop().then_inc(u_ready, 1)
            save(KTp[:, 2:4, :].rearrange("p a b -> p (a b)"), 512)
            own_evacs()
            ve.nop().then_inc(vcT_ready, 1)
            ve.wait_ge(gates_ready, 1)
            for c0, n, olo, ohi in ((0, 16, rq[:, :, :, 0:HALF], rq[:, :, :, HALF:ROPE]), (KS0, 4, None, None), (KW0, 4, None, None)):
                v = u[:, :, c0:c0 + n * DH].rearrange("p t (h d) -> p t h d", d=DH)
                lo, hi = v[:, :, :, 0:HALF], v[:, :, :, HALF:ROPE]
                rotate(lo, hi, lo if olo is None else olo, hi if ohi is None else ohi, n)
            for v, X in enumerate((KX, VX)):
                for q in shifted[4 * v:4 * v + 4]:
                    ve.wait_ge(q, 16)
                src = KT2[:, v, :, :].rearrange("p g (n j r) -> p j g n r", j=8, r=2)[:, :, :, :, 0]
                for half in range(2):
                    for g in range(GROUPS):
                        ins = ve.tensor_tensor(X[:, 8 * half:8 * half + 8, g, :], src[:, :, g, half:half + NCMP],
                                               pe_kv[:, v, 8 * half:8 * half + 8].unsqueeze(2).to_broadcast([P, 8, NCMP]), ALU.add)
            ins.then_inc(cmp_in_ready, 1)
            b = bank()
            freed(ve.tensor_copy(hidT[:, :, :, :].rearrange("p v k n -> p (v k n)"), ps[:, b, 0:4 * GROUPS * NCMP]))
            save(kcmpT[:, :], GROUPS * NCMP)
            b = bank()
            freed(ve.tensor_copy(vcmp[0:NCMP, :, :].rearrange("p g d -> p (g d)"), ps[0:NCMP, b, 0:GROUPS * DH]))
            own_evacs()
            afresh()
            sgv = sg[:, :, :].rearrange("p t (h b) -> p t h b", b=3)
            with t.loop(ve, 0, GROUPS, {dve_bank_full: 15, dve_bank_free: 15, dve_step: 13, scores_ready: 8, cmp_exp: 1}) as g:
                for half in range(2):
                    for tt in range(TT):
                        ve.tensor_copy(kk[:, tt, half * P:(half + 1) * P].rearrange("p (r d) -> p r d", r=2),
                                       u[:, tt, bass.ds(g * DH + (KS0, KW0)[half], DH)].unsqueeze(1).to_broadcast([P, 2, DH]))
                ve.tensor_copy(kcT[:, 0:NCMP], kcmpT[:, bass.ds(g * NCMP, NCMP)])
                ve.tensor_copy(vg[0:NCMP, :], vcmp[0:NCMP, bass.ds(g, 1), :].rearrange("p g d -> p (g d)"))
                for tt in range(TT):
                    ins = ve.tensor_copy(per_head(qr[:, tt, :])[:, :, 0:ROPE], rq[:, tt, bass.ds(g * 4, 4), :])
                ins.then_inc(dve_staged, 1)
                save(kT[:, :, :].rearrange("p a s -> p (a s)"), 512)
                sc4 = sc[:, :, :].rearrange("p (t h) n -> p t h n", t=TT)
                for par in range(2):
                    b = bank()
                    freed(ve.tensor_tensor(sc4[:, :, par:4:2, :],
                                           ps[:, b, 0:64].rearrange("p (t h n) -> p t h n", t=TT, h=2)[:, :, :, 0:NCMP],
                                           cmask[:, :, :].unsqueeze(2).to_broadcast([P, TT, 2, NCMP]), ALU.add))
                own_evacs()
                step(ve.tensor_reduce(cmx[:, 0, :], sc[:, :, :], AX, ALU.max))
                step(ve.tensor_scalar(cmx[:, 0, :], cmx[:, 0, :], -CLAMP, None, ALU.max))
                ve.tensor_tensor(sc[:, :, :], sc[:, :, :], cmx[:, 0, :].unsqueeze(2).to_broadcast([P, 8, NCMP]),
                                 ALU.subtract).then_inc(cmp_shifted, 1)

                def weights(inv, branch):
                    step(ve.tensor_tensor(coef[:, :].rearrange("p (t h) -> p t h", t=TT), inv.rearrange("p (t h) -> p t h", t=TT),
                                          sgv[:, :, bass.ds(g * 4, 4), branch], ALU.mult))

                def result_of(branch, into):
                    def result(tt, b):
                        if tt == 0:
                            weights(rinv[:, :], branch)
                        freed(ve.tensor_tensor(per_head(into[:, tt, :]), per_head(ps[:, b, 0:256]),
                                               wide_of(coef[:, 4 * tt:4 * tt + 4], 4), ALU.mult))
                    return result
                attend(True, result_of(1, yg))
                attend(True, result_of(2, yt))
                own_evacs()
                step(ve.tensor_tensor(yg[:, :, :], yg[:, :, :], yt[:, :, :], ALU.add))
                ve.wait_ge(cmp_exp, t.next(cmp_exp))
                step(ve.tensor_reduce(cmx[:, 1, :], ec[:, :, :], AX, ALU.add))
                step(ve.tensor_scalar(cmx[:, 1, :], cmx[:, 1, :], 1e-30, None, ALU.max))
                step(ve.reciprocal(cmx[:, 1, :], cmx[:, 1, :]))
                weights(cmx[:, 1, :], 0)
                for tt in range(TT):
                    b = bank()
                    freed(ve.tensor_copy(ecT[0:NCMP, 4 * tt:4 * tt + 4, :].rearrange("p h s -> p (h s)"), ps[0:NCMP, b, :]))
                for tt in range(TT):
                    b = bank()
                    step(ve.tensor_tensor(per_head(yt[:, tt, :]), per_head(ps[:, b, 0:256]), wide_of(coef[:, 4 * tt:4 * tt + 4], 4), ALU.mult))
                    freed(ve.tensor_tensor(h[:, tt, bass.ds(g * 256, 256)], yg[:, tt, :], yt[:, tt, :], ALU.add))
                heads_stand()
            afresh()
            heads_stand()
            turn_heads(0, KD)
            for c in range(2):
                for tt in range(TT):
                    add_x(tt, c)
            x_stands()
            cross(1)

            norm(xs)
            turn_h(5)
            b = bank()
            freed(ve.tensor_copy(logit[:, :, :].rearrange("p t e -> p (t e)"), ps[:, b, 0:TT * NE]))
            own_evacs()
            for tt in range(TT):
                step(ve.max(top[:, tt, :], logit[:, tt, :]))
                step(ve.max_index(topi[:, tt, :], top[:, tt, :], logit[:, tt, :]))
            ve.tensor_tensor(gap[:, 0, :], top[:, :, 1], top[:, :, 0], ALU.subtract).then_inc(gap_ready, 1)
            step(ve.tensor_copy(topf[:, :, :], topi[:, :, :]))
            for j in range(2):
                for tt in range(TT):
                    ins = ve.tensor_scalar(hot[:, j, tt, :], iota8, topf[:, tt, j:j + 1], None, ALU.is_equal)
            step(ins)
            ve.tensor_tensor(member[:, :, :], hot[:, 0], hot[:, 1], ALU.add).then_inc(members_ready, 1)
            ve.wait_ge(gap_exp, 1)
            step(ve.tensor_scalar(gap[:, 2, :], gap[:, 1, :], 1.0, None, ALU.add))
            step(ve.reciprocal(gap[:, 2, :], gap[:, 2, :]))
            step(ve.tensor_tensor(gap[:, 3, :], gap[:, 1, :], gap[:, 2, :], ALU.mult))
            for tt in range(TT):
                step(ve.tensor_scalar(gate[:, tt, 0:NE], hot[:, 0, tt, :], gap[:, 2, tt:tt + 1], None, ALU.mult))
                step(ve.scalar_tensor_tensor(gate[:, tt, 0:NE], hot[:, 1, tt, :], gap[:, 3, tt:tt + 1], gate[:, tt, 0:NE],
                                             ALU.mult, ALU.add))
            b = bank()
            for tt in range(TT):
                step(ve.scalar_tensor_tensor(rank[:, tt, 0:NE], ps[:, b, tt * NE:(tt + 1) * NE], 1.0, member[:, tt, :],
                                             ALU.add, ALU.mult))
            step(ve.tensor_scalar(rank[:, :, 0:NE], rank[:, :, 0:NE], -1.0, None, ALU.add))
            freed(ve.tensor_reduce(most[:, 0:1], ps[:, b, 2 * NE:3 * NE], AX, ALU.max))
            own_evacs()
            for j in range(1, 3):
                step(ve.tensor_scalar(rank[:, :, j * NE:(j + 1) * NE], rank[:, :, 0:NE], -float(P * j), None, ALU.add))
                step(ve.tensor_copy(gate[:, :, j * NE:(j + 1) * NE], gate[:, :, 0:NE]))
            step(ve.tensor_scalar(most[:, 1:2], most[:, 0:1], P + 0.5, float(NE), ALU.is_gt, ALU.mult))
            step(ve.tensor_scalar(most[:, 1:2], most[:, 1:2], float(NE), None, ALU.add))
            ve.tensor_copy(rounds[:, :], most[:, 1:2]).then_inc(routed, 1)
            ve.wait_ge(routed, 1)
            ve.wait_ge(gains_loaded, 16 * 2)
            for tt in range(TT):
                ins = ve.tensor_tensor(h[:, tt, :], h[:, tt, :], moe_g[:, :], ALU.mult)
            step(ins)
            n_it = ve.value_load(rounds[0:1, 0:1], min_val=NE, max_val=2 * NE)

            def choose(it):
                for tt in range(TT):
                    ins = ve.tensor_scalar(sel[:, tt, :], iota128[:, :], rank[:, tt, bass.ds(it, 1)], None, ALU.is_equal)
                ins.then_inc(sel_ready, 1)

            def save_x():
                ve.wait_ge(gathered, t.next(gathered))
                ve.tensor_copy(xT[:, 4:8, :].rearrange("p a b -> p (a b)"), ps[:, 3, :]).then_inc(xT_high_ready, 1)

            choose(0)
            save_x()

            def add_scattered():
                ve.wait_ge(scattered, t.next(scattered))
                for tt in range(TT):
                    part = xs[:, tt, :].rearrange("p (c n) -> p c n", c=2)
                    ins = ve.tensor_tensor(part, ps[:, (2, 6)[tt]:(2, 6)[tt] + 2, :], part, ALU.add)
                ins.then_inc(added, 1)
                t.next(added)

            with t.loop(ve, 0, n_it, {silu_ready: ESTEPS, up_full: ESTEPS, scattered: 1, added: 1, gathered: 1}) as it:
                for s in range(ESTEPS):
                    ve.wait_ge(silu_ready, t.next(silu_ready))
                    ve.wait_ge(up_full, t.next(up_full))
                    if s == ESTEPS - 1:
                        for tt in range(TT):
                            ve.tensor_scalar(selg[:, tt, :], iota128[:, :], rank[:, tt, bass.ds(it, 1)],
                                             gate[:, tt, bass.ds(it, 1)], ALU.is_equal, ALU.mult)
                    ve.tensor_tensor(act[:, :], ps[:, 5, :], sgate[:, :], ALU.mult).then_inc(act_ready, 1)
                    if s == 0:
                        add_scattered()
                choose(it + 1)
                save_x()
            add_scattered()
            ve.wait_ge(added, t.value(added))
            ve.nop().then_inc(x_ready, 1)
            norm(xs)
            ve.wait_ge(h_ready, t.value(h_ready))
            for tt in range(TT):
                ins = ve.tensor_tensor(h[:, tt, :], h[:, tt, :], fin_g[:, :], ALU.mult)
            ins.then_inc(out_ready, 1)


_INS = ["x", "mem", "positions", "norm_g", "mem_g", "final_g", "w_in_ab", "pool_w", "pool_scale", "w_out_ab",
        "ffn_w_gate", "ffn_w_up", "ffn_w_down", "w_in_c", "cmp_pe_k", "cmp_pe_v", "cmp_k_w1", "cmp_k_w2",
        "cmp_v_w1", "cmp_v_w2", "w_out_c", "router_w", "moe_w_gate", "moe_w_up", "moe_w_down", "xa_wq", "xa_wkv", "xa_wo"]


def kernel(**inputs):
    import numpy as _np
    import concourse.bacc as _bacc
    from concourse import mybir as _mybir
    from concourse.bass_utils import run_bass_kernel_spmd as _run

    nc = _bacc.Bacc("TRN2", target_bir_lowering=False, num_devices=1)
    arrays, args = {}, []
    for name in _INS:
        a = _np.ascontiguousarray(inputs[name])
        arrays[f"in_{name}"] = a
        args.append(nc.dram_tensor(f"in_{name}", a.shape, _mybir.dt.from_np(a.dtype), kind="ExternalInput").ap())
    o = nc.dram_tensor("out", (1, S, D), _mybir.dt.float32, kind="ExternalOutput").ap()
    build(nc, *args, o)
    r = _run(nc, [arrays], core_ids=[0])
    return r.results[0]["out"]
```

```python
import math
from contextlib import ExitStack, contextmanager

import numpy as np

import concourse.bass as bass
from concourse import mybir

F32 = mybir.dt.float32
F32R = mybir.dt.float32r
BF16 = mybir.dt.bfloat16
I32 = mybir.dt.int32
U32 = mybir.dt.uint32
ALU = mybir.AluOpType
ACT = mybir.ActivationFunctionType
AX = mybir.AxisListType.X

P = 128
D = 1024
S = 256
TT = S // P
KD = D // P
DH = 64
ROPE = 16
HALF = ROPE // 2
THETA = 500000.0
EPS = 1e-5
WINDOWS = (2, 4, 8, 16)
POOL = 256
MOBA = D - POOL
MOBA_UNITS = MOBA // 256
GROUPS = 4
CMP_LEN, CMP_STRIDE = 32, 16
NCMP = (S - CMP_LEN) // CMP_STRIDE + 1
CMP_HID = 256
KV = 256
C_IN = D + 6 * KV + 48
FF = 2816
FSTEP = 256
FSTEPS = FF // FSTEP
NE = 8
FFE = 3584
ESTEP = 512
ESTEPS = FFE // ESTEP
RING = 7
SLOT = 4096
PARTS = 4
PART = SLOT // PARTS
STAGES = 4
F_STAGES = 3
BIG = 1e30
CLAMP = 1e20
SCALE = DH ** -0.5
MAGIC = 1.5 * 2.0 ** 23
TWO_PI = (6.25, 0.03125, 63.0 / 32768.0)
TWO_PI_REST = 2 * math.pi - sum(TWO_PI)
KC0, VC0, KS0, VS0, KW0, VW0, GL0 = (D + i * KV for i in range(7))


class Tally:

    def __init__(self):
        self.n, self.i, self.per = {}, None, {}

    def value(self, sem):
        n = self.n.get(sem.name, 0)
        per = self.per.get(sem.name, 0)
        return n if self.i is None or not per else self.i * per + n

    def next(self, sem, k=1):
        self.n[sem.name] = self.n.get(sem.name, 0) + k
        return self.value(sem)

    @contextmanager
    def loop(self, eng, start, count, per):
        before = dict(self.n)
        self.per = {s.name: k for s, k in per.items()}
        if start:
            for s in self.per:
                self.n[s] = self.n.get(s, 0) - start * self.per[s]
        with eng.Fori(start, count) as i:
            self.i = i
            yield i
        if start:
            for s in self.per:
                self.n[s] += start * self.per[s]
        got = {s: self.n[s] - before.get(s, 0) for s in self.n if self.n[s] - before.get(s, 0)}
        assert got == {s: k for s, k in self.per.items() if k}, (got, self.per)
        self.i = None
        for s, k in self.per.items():
            self.n[s] = (count - start) * k + before.get(s, 0)
        self.per = {}


def build(nc, x, mem, positions, norm_g, mem_g, final_g, w_in_ab, pool_w, pool_scale, w_out_ab,
          ffn_w_gate, ffn_w_up, ffn_w_down, w_in_c, cmp_pe_k, cmp_pe_v, cmp_k_w1, cmp_k_w2,
          cmp_v_w1, cmp_v_w2, w_out_c, router_w, moe_w_gate, moe_w_up, moe_w_down,
          xa_wq, xa_wkv, xa_wo, out):
    ctx = ExitStack()
    with ctx:
        def sb(name, shape, dt=F32):
            return ctx.enter_context(nc.sbuf_tensor(name, shape, dt))

        def sem(name):
            return ctx.enter_context(nc.semaphore(name))

        ring = sb("ring", [P, RING, SLOT])
        xs = sb("xs", [P, TT, D])
        h = sb("h", [P, TT, D])
        ident = sb("ident", [P, P])
        identb = sb("identb", [P, P], BF16)
        causal = sb("causal", [P, 2 * P], BF16)
        cmask = sb("cmask", [P, TT, NCMP])
        zeros = sb("zeros", [P, 2 * P])
        band = sb("band", [P, 4, TT, S])
        before = sb("before", [P, P])
        ones = sb("ones", [P, P])
        iota128 = sb("iota128", [P, P])
        iota8 = iota128[:, 0:NE]
        NROWS = 7 * KD + 2 + 2 * 16
        small = sb("small", [P, NROWS])
        gT = small[:, 0:7 * KD].rearrange("p (g k) -> p g k", g=7)
        pscale = small[:, 7 * KD:7 * KD + 2]
        pe_kv = small[:, 7 * KD + 2:NROWS].rearrange("p (v j) -> p v j", v=2)
        pw = sb("pw", [P, 2, DH])
        w2 = sb("w2", [P, 2, 2, DH])
        rw = sb("rw", [P, KD, NE])
        pos_i = sb("pos_i", [P, TT], I32)
        pos = sb("pos", [P, TT])
        eps = sb("eps", [P, 1])
        half_pi = sb("half_pi", [P, 1])
        ang = sb("ang", [P, TT, HALF])
        red = sb("red", [P, 2, TT, HALF])
        cos = sb("cos", [P, TT, HALF])
        sin = sb("sin", [P, TT, HALF])
        ss = sb("ss", [P, TT])
        rms = sb("rms", [P, TT])
        rstd = sb("rstd", [P, TT])
        nmax = sb("nmax", [P, 8])
        rsum = sb("rsum", [P, 8])
        rinv = sb("rinv", [P, 8])
        coef = sb("coef", [P, 8])
        sg = sb("sg", [P, TT, 48])
        kcT = sb("kcT", [P, 2 * NE])
        kcmpT = sb("kcmpT", [P, GROUPS * NCMP])
        vcmp = sb("vcmp", [16, GROUPS, DH])
        vg = sb("vg", [16, DH])
        hidT = sb("hidT", [P, 2, 2, GROUPS * NCMP])
        sc = sb("sc", [P, 8, NCMP])
        ec = sb("ec", [P, 8, NCMP])
        cmx = sb("cmx", [P, 3, 8])
        logit = sb("logit", [P, TT, NE])
        top = sb("top", [P, TT, 8])
        topi = sb("topi", [P, TT, 8], U32)
        topf = sb("topf", [P, TT, 8])
        hot = sb("hot", [P, 2, TT, NE])
        member = sb("member", [P, TT, NE])
        gap = sb("gap", [P, 4, TT])
        gate = sb("gate", [P, TT, 3 * NE])
        rank = sb("rank", [P, TT, 3 * NE])
        most = sb("most", [P, 2])
        rounds = sb("rounds", [P, 1], I32)
        trunk = ExitStack()

        def early(name, shape, dt=F32):
            return trunk.enter_context(nc.sbuf_tensor(name, shape, dt))

        hT = early("hT", [P, KD, S])
        kvm = early("kvm", [P, 2, TT, 512])
        attention = ExitStack()

        def heads_(name, shape):
            return attention.enter_context(nc.sbuf_tensor(name, shape, F32))

        u = heads_("u", [P, TT, C_IN])
        qr = heads_("qr", [P, TT, 256])
        kk = heads_("kk", [P, TT, 256])
        qT = heads_("qT", [P, 2, S])
        kT = heads_("kT", [P, 2, S])
        prob = heads_("prob", [P, TT, 4, S])
        pT = heads_("pT", [P, 4, 512])
        flat_band = band[:, :, :, :].rearrange("p a b c -> p (a b c)")
        rq = flat_band[:, 0:512].rearrange("p (t h r) -> p t h r", t=TT, h=16)
        yg = flat_band[:, 512:1024].rearrange("p (t c) -> p t c", t=TT)
        yt = flat_band[:, 1024:1536].rearrange("p (t c) -> p t c", t=TT)
        qc = yt
        qcT = yg[:, :, :]
        pooled = kT
        hid = flat_band[0:64, 1536:2048].rearrange("p (t c) -> p t c", t=2)
        moe_g, fin_g = flat_band[:, 0:D], flat_band[:, D:2 * D]
        rt = hT[:, 2:8, :].rearrange("p a b -> p (a b)").rearrange("p (j t h r) -> p j t h r", j=4, t=TT, h=24)
        ecT = prob[0:16, 0, :, :].rearrange("p a b -> p (a b)").rearrange("p (h s) -> p h s", h=8)
        mem_x = u[:, :, 0:D]
        small_rows = u[:, 0, D:D + P]
        sgate, act = h[:, 0, 0:512], h[:, 0, 512:1024]
        KTp = prob[:, :, :, :].rearrange("p a b c -> p (a b) c")[:, 0:4, :]
        KT2 = pT[:, :, :].rearrange("p a b -> p (a b)").rearrange("p (v g t) -> p v g t", v=2, g=GROUPS)
        KX = hT[:, :, :].rearrange("p a b -> p (a b)")[:, 0:16 * 60].rearrange("p (j g n) -> p j g n", j=16, g=GROUPS)
        VX = hT[:, :, :].rearrange("p a b -> p (a b)")[:, 1024:1024 + 16 * 60].rearrange(
            "p (j g n) -> p j g n", j=16, g=GROUPS)

        attention.close()
        swiglu = ExitStack()

        def split(name, shape):
            return swiglu.enter_context(nc.sbuf_tensor(name, shape, F32R))

        f_w_hi, f_w_lo = split("f_w_hi", [P, F_STAGES, PART]), split("f_w_lo", [P, F_STAGES, PART])
        h_hi, h_lo = split("h_hi", [P, KD, S]), split("h_lo", [P, KD, S])
        aT_hi, aT_lo = split("aT_hi", [P, 4 * P]), split("aT_lo", [P, 4 * P])
        swiglu.close()
        trunk.close()
        w_hi = sb("w_hi", [P, STAGES, PART], F32R)
        w_lo = sb("w_lo", [P, STAGES, PART], F32R)
        x_hi = sb("x_hi", [P, KD, P], F32R)
        x_lo = sb("x_lo", [P, KD, P], F32R)
        a_hi = sb("a_hi", [P, 4, P], F32R)
        a_lo = sb("a_lo", [P, 4, P], F32R)
        e_act = sb("e_act", [P, ESTEP])
        e_gate = sb("e_gate", [P, ESTEP])
        outE = sb("outE", [P, D])
        sel = sb("sel", [P, TT, P])
        selg = sb("selg", [P, TT, P])
        selT = sb("selT", [P, S])

        ps = ctx.enter_context(nc.psum_tensor("ps", [P, 8, 512], F32))

        loads = [sem(f"loaded_{n}") for n in ("x", "mem", "small", "late")]
        x_loaded, mem_loaded, small_loaded, late_loaded = loads
        pool_step = sem("pool_step")
        consts_ready = sem("consts_ready")
        weights_ready = [sem(f"weights_ready_{i}") for i in range(RING)]
        weights_used = sem("weights_used")
        act_bank_full, act_bank_free = sem("act_bank_full"), sem("act_bank_free")
        scores_ready, probs_ready = sem("scores_ready"), sem("probs_ready")
        dve_bank_full, dve_bank_free = sem("dve_bank_full"), sem("dve_bank_free")
        nmax_ready = sem("nmax_ready")
        dve_step, act_step = sem("dve_step"), sem("act_step")
        x_ready, rms_ready, h_ready = sem("x_ready"), sem("rms_ready"), sem("h_ready")
        angles_ready, tables_ready = sem("angles_ready"), sem("tables_ready")
        act_staged, dve_staged = sem("act_staged"), sem("dve_staged")
        gains_loaded = sem("gains_loaded")
        rows_loaded, small_ready = sem("rows_loaded"), sem("small_ready")
        band_counted = sem("band_counted")
        counts_ready = sem("counts_ready")
        u_ready = sem("u_ready")
        heads_ready = sem("heads_ready")
        shifted = [sem(f"shifted_{i}") for i in range(8)]
        vcT_ready = sem("vcT_ready")
        cmp_in_ready = sem("cmp_in_ready")
        gates_ready = sem("gates_ready")
        cmp_shifted, cmp_exp = sem("cmp_shifted"), sem("cmp_exp")
        hi_ready, lo_ready = sem("hi_ready"), sem("lo_ready")
        part_used = sem("part_used")
        e_silu_ready, e_act_ready, e_turned = sem("e_silu_ready"), sem("e_act_ready"), sem("e_turned")
        a_hi_ready, a_lo_ready = sem("a_hi_ready"), sem("a_lo_ready")
        x_hi_ready, x_lo_ready = sem("x_hi_ready"), sem("x_lo_ready")
        silu_ready, act_ready = sem("silu_ready"), sem("act_ready")
        turned, aT_hi_ready, aT_lo_ready = sem("turned"), sem("aT_hi_ready"), sem("aT_lo_ready")
        hT_stands, h_hi_ready, h_lo_ready = sem("hT_stands"), sem("h_hi_ready"), sem("h_lo_ready")
        f_hi_ready, f_lo_ready = sem("f_hi_ready"), sem("f_lo_ready")
        f_part_used = sem("f_part_used")
        ffn_added = sem("ffn_added")
        down_saved = sem("down_saved")
        gap_ready, gap_exp, members_ready, routed = sem("gap_ready"), sem("gap_exp"), sem("members_ready"), sem("routed")
        sel_ready, gathered = sem("sel_ready"), sem("gathered")
        selT_full, selT_ready = sem("selT_full"), sem("selT_ready")
        scattered, added = sem("scattered"), sem("added")
        out_ready, stored = sem("out_ready"), sem("stored")

        def cols(w, c0, n):
            return w[:, c0:c0 + n].rearrange("(k p) n -> p k n", p=P)

        def rows(w, r0, k):
            return w[bass.ds(r0, k * P), :].rearrange("(k p) n -> p k n", p=P)

        def slot_cols(slot, n):
            return ring[:, slot, :].rearrange("p (k n) -> p k n", k=KD)[:, :, 0:n]

        def slot_rows(slot, k):
            return ring[:, slot, 0:k * D].rearrange("p (k n) -> p k n", k=k)

        HEAD_UNITS = ([("c", xa_wkv[i], 0, 512) for i in range(2)]
                      + [("c", w_in_ab[0], 512 * j, 512) for j in range(5)]
                      + [("c", w_out_ab[0], 512 * j, 512) for j in range(2)]
                      + [("c", xa_wq[0], 0, 256), ("r", xa_wo[0], 0, 2)])
        IN_C = [(512 * j, min(512, C_IN - 512 * j)) for j in range(6)]
        MID_UNITS = ([("c", w_in_c[0], c0, n) for c0, n in IN_C]
                     + [("w", cmp_k_w1[0], 0, 16), ("w", cmp_v_w1[0], 0, 16)]
                     + [("c", w_out_c[0], 512 * j, 512) for j in range(2)]
                     + [("c", xa_wq[1], 0, 256), ("r", xa_wo[1], 0, 2)])
        FFN_FIRST = len(HEAD_UNITS)
        FFN_LOOP = FFN_FIRST + 1
        FFN_LAST = FFN_LOOP + 4
        MID_FIRST = FFN_LAST + 1
        MOE_FIRST = MID_FIRST + len(MID_UNITS)
        MOE_ORDER = [("g", 0), ("u", 0)]
        for s in range(1, ESTEPS):
            MOE_ORDER += [("g", s), ("u", s), ("d", s - 1)]
        MOE_ORDER += [("d", ESTEPS - 1)]
        assert len(MOE_ORDER) % RING == 0 and (FSTEPS - 1) % 2 == 0

        SLOTS = {ks: (MOE_FIRST + j) % RING for j, ks in enumerate(MOE_ORDER)}
        NPARTS = PARTS * len(MOE_ORDER)
        head_loads, mid_loads, trunk_loads = {}, {}, {}

        def raw(slot, part):
            return ring[:, slot, part * PART:(part + 1) * PART]

        block = ctx.enter_context(nc.Block())

        @block.sync
        def _(sp):
            t = Tally()

            def load(slot, dsts_srcs, depth):
                slot %= RING
                n = t.value(weights_used)
                if t.i is not None or n - depth + 2 > 0:
                    if t.i is not None or n >= depth:
                        sp.wait_ge(weights_used, n - depth + 2)
                t.next(weights_used)
                for dst, src in dsts_srcs(slot):
                    sp.dma_start(dst, src).then_inc(weights_ready[slot], 16)
                    t.next(weights_ready[slot], 16)

            def plain(unit):
                kind, w, at, n = unit
                if kind == "c":
                    return lambda s: [(slot_cols(s, n), cols(w, at, n))]
                if kind == "r":
                    return lambda s: [(slot_rows(s, n), rows(w, at, n))]
                return lambda s: [(ring[:, s, :].rearrange("p (k n) -> p k n", k=16), w.rearrange("(k p) n -> p k n", p=P))]

            def gate_up(c):
                return lambda s: [(slot_cols(s, 2 * FSTEP)[:, :, j * FSTEP:(j + 1) * FSTEP],
                                   w[0][:, bass.ds(c, FSTEP)].rearrange("(k p) n -> p k n", p=P))
                                  for j, w in enumerate((ffn_w_gate, ffn_w_up))]

            def down(r):
                return lambda s: [(slot_rows(s, 2), rows(ffn_w_down[0], r, 2))]

            sp.wait_ge(mem_loaded, 16)
            for j, unit in enumerate(HEAD_UNITS):
                load(j, plain(unit), RING)
            head_loads.update(t.n)
            load(FFN_FIRST, gate_up(0), RING)
            per = {weights_ready[(FFN_LOOP + j) % RING]: (32, 16)[j % 2] for j in range(4)}
            with t.loop(sp, 0, (FSTEPS - 1) // 2, {**per, weights_used: 4}) as i:
                for j in range(2):
                    load(FFN_LOOP + 2 * j, gate_up(i * (2 * FSTEP) + (j + 1) * FSTEP), 4)
                    load(FFN_LOOP + 2 * j + 1, down(i * (2 * FSTEP) + j * FSTEP), 4)
            load(FFN_LAST, down(FF - FSTEP), RING)
            mid_loads.update(t.n)
            for j, unit in enumerate(MID_UNITS):
                load(MID_FIRST + j, plain(unit), RING)

            trunk_loads.update(t.n)

            def expert(e):
                def of(w):
                    return w[0, bass.ds(e, 1)].rearrange("e r c -> (e r) c")
                for j, (kind, s) in enumerate(MOE_ORDER):
                    if t.i is None and j < RING:
                        sp.wait_ge(weights_used, MOE_FIRST_UNIT + j - RING + 2)
                    else:
                        sp.wait_ge(lo_ready, t.value(lo_ready) - PARTS * (RING - 1))
                    t.next(lo_ready, PARTS)
                    slot = SLOTS[kind, s]
                    if kind == "d":
                        dst = slot_rows(slot, 4)
                        src = of(moe_w_down)[s * ESTEP:(s + 1) * ESTEP, :].rearrange("(k p) n -> p k n", p=P)
                    else:
                        dst = slot_cols(slot, ESTEP)
                        src = cols(of(moe_w_gate if kind == "g" else moe_w_up), s * ESTEP, ESTEP)
                    sp.dma_start(dst, src).then_inc(weights_ready[slot], 16)

            MOE_FIRST_UNIT = t.value(weights_used)
            expert(0)
            sp.wait_ge(routed, 1)
            n_it = sp.value_load(rounds[0:1, 0:1], min_val=NE, max_val=2 * NE)
            with t.loop(sp, 1, n_it, {lo_ready: NPARTS}) as it:
                expert(it % NE)
            sp.wait_ge(out_ready, 1)
            sp.dma_start(out[0].rearrange("(t p) d -> p t d", p=P), h[:, :, :]).then_inc(stored, 16)
            sp.wait_ge(stored, 16)

        @block.gpsimd
        def _(pool):
            steps = [0]

            def step(ins):
                ins.then_inc(pool_step, 1)
                steps[0] += 1
                pool.wait_ge(pool_step, steps[0])

            step(pool.memset(zeros[:, :], 0.0))
            step(pool.memset(eps[:, :], EPS))
            step(pool.memset(half_pi[:, :], math.pi / 2))
            step(pool.affine_select(out=ident[:, :], in_=zeros[:, 0:P], compare_op=ALU.not_equal, fill=1.0,
                                    base=0, pattern=[[-1, P]], channel_multiplier=1))
            pool.nop().then_inc(consts_ready, 1)
            for g, w in enumerate(WINDOWS):
                step(pool.iota(band[:, g, :, :], [[0, TT], [1, S]], base=1, channel_multiplier=0,
                               allow_small_or_imprecise_dtypes=True))
                step(pool.tensor_scalar(band[:, g, :, :], band[:, g, :, :], float(w), None, ALU.min))
            pool.nop().then_inc(band_counted, 1)
            step(pool.memset(ones[:, :], 1.0))
            step(pool.affine_select(out=identb[:, :], in_=zeros[:, 0:P], compare_op=ALU.not_equal, fill=1.0,
                                    base=0, pattern=[[-1, P]], channel_multiplier=1))
            step(pool.affine_select(out=causal[:, :], in_=zeros[:, :], compare_op=ALU.is_ge, fill=-BIG,
                                    base=P, pattern=[[-1, 2 * P]], channel_multiplier=1))
            step(pool.affine_select(out=cmask[:, :, :], in_=zeros[:, 0:TT * NCMP].rearrange("p (t n) -> p t n", t=TT),
                                    compare_op=ALU.is_ge, fill=-BIG, base=-(CMP_LEN - 1),
                                    pattern=[[P, TT], [-CMP_STRIDE, NCMP]], channel_multiplier=1))
            step(pool.affine_select(out=before[:, :], in_=zeros[:, 0:P], compare_op=ALU.is_ge, fill=1.0,
                                    base=0, pattern=[[-1, P]], channel_multiplier=1))
            step(pool.iota(iota128[:, :], [[1, P]], base=0, channel_multiplier=0, allow_small_or_imprecise_dtypes=True))
            pool.wait_ge(counts_ready, 1)
            for g, w in enumerate(WINDOWS):
                step(pool.affine_select(out=band[:, g, :, :], in_=band[:, g, :, :], compare_op=ALU.is_ge, fill=0.0,
                                        base=0, pattern=[[-P, TT], [1, S]], channel_multiplier=-1))
                step(pool.affine_select(out=band[:, g, :, :], in_=band[:, g, :, :], compare_op=ALU.is_ge, fill=0.0,
                                        base=w - 1, pattern=[[P, TT], [-1, S]], channel_multiplier=1))
            for g in range(4):
                for tt in range(TT):
                    step(pool.tensor_tensor(band[:, g, tt, tt * P:(tt + 1) * P], band[:, g, tt, tt * P:(tt + 1) * P],
                                            ident[:, :], ALU.subtract))
            pool.nop().then_inc(consts_ready, 1)
            pool.wait_ge(heads_ready, MOBA_UNITS + 1 + 1 + GROUPS + 1)
            pool.dma_start(moe_g, norm_g[1, 2].partition_broadcast(P)).then_inc(gains_loaded, 16)
            pool.dma_start(fin_g, final_g.partition_broadcast(P)).then_inc(gains_loaded, 16)

        @block.tensor
        def _(pe):
            t = Tally()
            local = {}
            first = {}
            units = [0]

            def bank(full, free, base):
                k = local.get(full.name, 0)
                local[full.name] = k + 1
                n = t.value(full)
                if k < 2:
                    need = first.get(full.name, 0)
                else:
                    need = n - 1
                if not isinstance(need, int) or need > 0:
                    pe.wait_ge(free, need)
                return base + k % 2

            def act_bank():
                return bank(act_bank_full, act_bank_free, 0)

            def score_bank():
                return bank(scores_ready, probs_ready, 2)

            def dve_bank():
                return bank(dve_bank_full, dve_bank_free, 6)

            def afresh():
                for s in (act_bank_full, scores_ready, dve_bank_full):
                    local[s.name] = 0
                    first[s.name] = t.value(s)

            def emptied():
                for full, free in ((act_bank_full, act_bank_free), (dve_bank_full, dve_bank_free)):
                    n = t.value(full)
                    if not isinstance(n, int) or n > 0:
                        pe.wait_ge(free, n)

            def unit(slot, loads=1):
                s = weights_ready[slot % RING]
                pe.wait_ge(s, t.next(s, 16 * loads))
                return slot % RING

            def project(src, slot, n, where, group=KD):
                w = slot_cols(unit(slot), n)
                for tt in range(TT):
                    full = where[tt]
                    b = act_bank() if full is act_bank_full else dve_bank()
                    for k in range(KD):
                        mm = pe.matmul(ps[:, b, 0:n], src[:, k, tt * P:(tt + 1) * P], w[:, k, :],
                                       start=(k == 0), stop=(k == KD - 1))
                        if tt == 0 and k == 0:
                            mm.then_inc(weights_used, 1)
                    mm.then_inc(full, 1)
                    t.next(full)

            def turn(blocks, full, width=P, rows_=P):
                b = act_bank() if full is act_bank_full else dve_bank()
                for j, blk in enumerate(blocks):
                    mm = pe.transpose(ps[0:width, b, j * rows_:(j + 1) * rows_], blk, ident[0:rows_, 0:rows_])
                mm.then_inc(full, 1)
                t.next(full)

            def turn_h():
                pe.wait_ge(h_ready, t.next(h_ready))
                for j in range(KD // 2):
                    turn([h[:, tt, k * P:(k + 1) * P] for k in (2 * j, 2 * j + 1) for tt in range(TT)],
                         act_bank_full if j % 2 == 0 else dve_bank_full)
                emptied()

            def turn_heads(n, full_of=lambda j: act_bank_full if j % 2 == 0 else dve_bank_full):
                pe.wait_ge(heads_ready, t.next(heads_ready))
                for j in range(n // 2):
                    turn([h[:, tt, k * P:(k + 1) * P] for k in (2 * j, 2 * j + 1) for tt in range(TT)], full_of(j))
                emptied()

            def attend(q, k_of, v_of, is_causal):
                for tt in range(TT):
                    keys = P if is_causal and tt == 0 else S
                    for par in range(2):
                        half = slice(par * DH, (par + 1) * DH)
                        b = score_bank()
                        if is_causal:
                            pe.matmul(ps[:, b, 0:2 * keys].rearrange("p (h k) -> p h k", h=2), identb[:, :],
                                      causal[:, 2 * P - keys:2 * P].unsqueeze(1).to_broadcast([P, 2, keys]),
                                      start=True, stop=False, skip_group_check=True)
                        for j in range(2):
                            mm = pe.matmul(ps[:, b, j * keys:(j + 1) * keys], q[half, j, tt * P:(tt + 1) * P],
                                           k_of(2 * j + par, half)[:, 0:keys], start=not is_causal, stop=True,
                                           skip_group_check=True)
                        mm.then_inc(scores_ready, 1)
                        t.next(scores_ready)
                blocks = [(tt, kc) for tt in range(TT) for kc in range(TT) if not is_causal or kc <= tt]
                pe.wait_ge(probs_ready, t.value(scores_ready))
                for j, (tt, kc) in enumerate(blocks):
                    turn([prob[:, tt, hd, kc * P:(kc + 1) * P] for hd in range(4)],
                         act_bank_full if j % 2 else dve_bank_full)
                emptied()
                for tt in range(TT):
                    b = dve_bank()
                    mine = [(j, kc) for j, (a, kc) in enumerate(blocks) if a == tt]
                    for hd in range(4):
                        for n, (j, kc) in enumerate(mine):
                            mm = pe.matmul(ps[:, b, hd * DH:(hd + 1) * DH], pT[:, j, hd * P:(hd + 1) * P], v_of(kc, hd),
                                           start=(n == 0), stop=(n == len(mine) - 1))
                    mm.then_inc(dve_bank_full, 1)
                    t.next(dve_bank_full)

            def pairs(stage):
                return [stage[:, tt, pr * P:(pr + 1) * P] for pr in range(2) for tt in range(TT)]

            def cross(layer, slot):
                turn_h()
                project(hT, slot, 256, (act_bank_full, dve_bank_full))
                emptied()
                turn(pairs(qr), act_bank_full)
                turn([kvm[:, layer, tt, pr * P:(pr + 1) * P] for pr in range(2) for tt in range(TT)], dve_bank_full)
                emptied()
                attend(qT, lambda hd, half: kT[half, hd // 2, :],
                       lambda kc, hd: kvm[:, layer, kc, 256 + hd * DH:256 + (hd + 1) * DH], False)
                turn_heads(2)
                w = slot_rows(unit(slot + 1), 2)
                for tt in range(TT):
                    for c in range(2):
                        b = dve_bank()
                        for k in range(2):
                            mm = pe.matmul(ps[:, b, :], hT[:, k, tt * P:(tt + 1) * P], w[:, k, c * 512:(c + 1) * 512],
                                           start=(k == 0), stop=(k == 1))
                            if tt == c == k == 0:
                                mm.then_inc(weights_used, 1)
                        mm.then_inc(dve_bank_full, 1)
                        t.next(dve_bank_full)

            pe.wait_ge(consts_ready, 1)
            pe.wait_ge(rows_loaded, 16 * 5)
            turn([small_rows[0:NROWS, :]], dve_bank_full, P, NROWS)
            turn_h()
            for layer in range(2):
                project(hT, layer, 512, (act_bank_full, dve_bank_full))
            turn_h()
            for j in range(5):
                project(hT, 2 + j, 512, (act_bank_full, dve_bank_full))
            emptied()
            pe.wait_ge(consts_ready, 2)
            pe.wait_ge(small_loaded, t.next(small_loaded, 16 * 4))
            for pr in range(2):
                b = dve_bank()
                for g in (2 * pr, 2 * pr + 1):
                    at = (g % 2) * DH
                    for st in range(TT):
                        mm = pe.matmul(ps[at:at + DH, b, 0:S], u[:, st, g * DH:(g + 1) * DH], band[:, g, st, :],
                                       start=(st == 0), stop=(st == TT - 1))
                mm.then_inc(dve_bank_full, 1)
                t.next(dve_bank_full)
            emptied()
            for pr in range(2):
                b = dve_bank()
                for j in range(2):
                    half = slice(j * DH, (j + 1) * DH)
                    mm = pe.matmul(ps[half, b, 0:S], pw[half, pr, :], pooled[half, pr, :], start=True, stop=True)
                mm.then_inc(dve_bank_full, 1)
                t.next(dve_bank_full)
            afresh()
            with t.loop(pe, 0, MOBA_UNITS, {act_staged: 1, dve_staged: 1, act_bank_full: 2, dve_bank_full: 5,
                                            scores_ready: 4, heads_ready: 1}) as i:
                t.next(heads_ready)
                first.update({s.name: t.value(s) for s in (act_bank_full, scores_ready, dve_bank_full)})
                pe.wait_ge(act_staged, t.next(act_staged))
                pe.wait_ge(dve_staged, t.next(dve_staged))
                turn(pairs(qr), act_bank_full)
                turn(pairs(kk), dve_bank_full)
                emptied()
                attend(qT, lambda hd, half: kT[half, hd // 2, :],
                       lambda kc, hd: u[:, kc, bass.ds(i * 256 + (POOL + 2 * MOBA + hd * DH), DH)], True)
            afresh()
            turn_heads(MOBA // P)
            for j in range(2):
                project(hT, 7 + j, 512, (dve_bank_full, dve_bank_full))
            cross(0, 9)

            turn_h()

            for b in range(4):
                for c in range(2):
                    pe.matmul(ps[:, b, c * 256:(c + 1) * 256], zeros[:, 0:P], zeros[:, :], start=True, stop=False,
                              skip_group_check=True)
            pe.wait_ge(h_hi_ready, KD // 2)
            pe.wait_ge(h_lo_ready, KD // 2)

            def products(bnk, hi, lo, w_h, w_l, start, stop):
                first_ = pe.matmul(ps[:, bnk, :], hi, w_h, start=start, stop=False, skip_group_check=True)
                pe.matmul(ps[:, bnk, :], lo, w_h, start=False, stop=False, skip_group_check=True)
                return first_, pe.matmul(ps[:, bnk, :], hi, w_l, start=False, stop=stop, skip_group_check=True)

            def f_part(slot, is_first, terms):
                pe.wait_ge(f_lo_ready, t.next(f_lo_ready))
                st = f_part.k % F_STAGES
                f_part.k += 1
                for n, (bnk, hi, lo, at, start, stop) in enumerate(terms):
                    one, mm = products(bnk, hi, lo, f_w_hi[:, st, at:at + 512], f_w_lo[:, st, at:at + 512], start, stop)
                    if n == 0 and is_first:
                        one.then_inc(weights_used, 1)
                mm.then_inc(f_part_used, 1)
                t.next(f_part_used)
                return mm
            f_part.k = 0

            def gate_up(slot, parts):
                if parts[0] == 0:
                    n = t.value(act_ready)
                    if t.i is not None or n > 0:
                        pe.wait_ge(act_ready, n)
                for q in parts:
                    at = [slice(tt * P, (tt + 1) * P) for tt in range(TT)]
                    mm = f_part(slot, q == 0, [
                        (4 + tt, h_hi[:, k, at[tt]], h_lo[:, k, at[tt]], (k % 2) * 512,
                         k == 0, k == KD - 1) for tt in range(TT) for k in (2 * q, 2 * q + 1)])
                if parts[-1] == PARTS - 1:
                    t.next(act_ready, TT)

            def turn_act():
                pe.wait_ge(act_ready, t.value(act_ready))
                for kc in range(2):
                    for tt in range(TT):
                        mm = pe.transpose(ps[:, 6, (kc * TT + tt) * P:(kc * TT + tt + 1) * P],
                                          act[:, tt * FSTEP + kc * P:tt * FSTEP + (kc + 1) * P], ident[:, :])
                mm.then_inc(turned, 1)
                t.next(turned)

            def down(slot, stop):
                pe.wait_ge(aT_hi_ready, t.value(turned))
                pe.wait_ge(aT_lo_ready, t.value(turned))
                for kc in range(2):
                    at = [slice((kc * TT + tt) * P, (kc * TT + tt + 1) * P) for tt in range(TT)]
                    mm = f_part(slot, kc == 0, [(2 * tt + c, aT_hi[:, at[tt]], aT_lo[:, at[tt]], c * 512, False,
                                                 stop and kc == 1) for tt in range(TT) for c in range(2)])

            gate_up(FFN_FIRST, range(PARTS))
            with t.loop(pe, 0, (FSTEPS - 1) // 2, {f_lo_ready: 12, f_part_used: 12, act_ready: 4, turned: 2}) as i:
                for j in range(2):
                    gate_up(FFN_LOOP + 2 * j, (0,))
                    turn_act()
                    gate_up(FFN_LOOP + 2 * j, (1, 2, 3))
                    down(FFN_LOOP + 2 * j + 1, False)
            turn_act()
            down(FFN_LAST, True)
            t.n.update(mid_loads)
            pe.wait_ge(ffn_added, 1)

            turn_h()
            for j, (c0, n) in enumerate(IN_C):
                project(hT, MID_FIRST + j, n, (act_bank_full, dve_bank_full))
            emptied()
            for c0 in (KC0, VC0):
                turn([u[:, tt, c0 + pr * P:c0 + (pr + 1) * P] for pr in range(2) for tt in range(TT)],
                     act_bank_full if c0 == KC0 else dve_bank_full)
            pe.wait_ge(cmp_in_ready, t.next(cmp_in_ready))
            for v, X in enumerate((KX, VX)):
                s = unit(MID_FIRST + len(IN_C) + v)
                w = ring[:, s, :].rearrange("p (k n) -> p k n", k=16)
                b = act_bank()
                for j in range(16):
                    mm = pe.matmul(ps[0:GROUPS * NCMP, b, 0:CMP_HID], X[:, j].rearrange("p g n -> p (g n)"), w[:, j, :],
                                   start=(j == 0), stop=(j == 15))
                    if j == 0:
                        mm.then_inc(weights_used, 1)
                mm.then_inc(act_bank_full, 1)
                t.next(act_bank_full)
            emptied()
            turn([hid[0:GROUPS * NCMP, v, kc * P:(kc + 1) * P] for v in range(2) for kc in range(2)],
                 dve_bank_full, P, GROUPS * NCMP)
            emptied()
            b = dve_bank()
            for at in (0, DH):
                for kc in range(2):
                    mm = pe.matmul(ps[at:at + DH, b, 0:GROUPS * NCMP], w2[:, 0, kc, :], hidT[:, 0, kc, :],
                                   start=(kc == 0), stop=(kc == 1))
            mm.then_inc(dve_bank_full, 1)
            t.next(dve_bank_full)
            b = dve_bank()
            for g in range(GROUPS):
                for kc in range(2):
                    mm = pe.matmul(ps[0:NCMP, b, g * DH:(g + 1) * DH], hidT[:, 1, kc, g * NCMP:(g + 1) * NCMP],
                                   w2[:, 1, kc, :], start=(kc == 0), stop=(kc == 1))
            mm.then_inc(dve_bank_full, 1)
            t.next(dve_bank_full)
            afresh()
            with t.loop(pe, 0, GROUPS, {act_staged: 1, dve_staged: 1, act_bank_full: 4, dve_bank_full: 15,
                                        scores_ready: 8, cmp_exp: 1, heads_ready: 1}) as g:
                t.next(heads_ready)
                first.update({s.name: t.value(s) for s in (act_bank_full, scores_ready, dve_bank_full)})
                pe.wait_ge(act_staged, t.next(act_staged))
                pe.wait_ge(dve_staged, t.next(dve_staged))
                turn(pairs(qr), act_bank_full)
                turn(pairs(kk), dve_bank_full)
                turn(pairs(qc), act_bank_full)
                emptied()
                for par in range(2):
                    b = dve_bank()
                    half = slice(par * DH, (par + 1) * DH)
                    for tt in range(TT):
                        for j in range(2):
                            c = (tt * 2 + j) * 16
                            mm = pe.matmul(ps[:, b, c:c + NCMP], qcT[half, j, tt * P:(tt + 1) * P], kcT[half, 0:NCMP],
                                           start=True, stop=True)
                    mm.then_inc(dve_bank_full, 1)
                    t.next(dve_bank_full)
                for which, v0 in enumerate((VS0, VW0)):
                    attend(qT, lambda hd, half: kT[half, which, :],
                           lambda kc, hd: u[:, kc, bass.ds(g * DH + v0, DH)], True)
                pe.wait_ge(cmp_exp, t.next(cmp_exp))
                for tt in range(TT):
                    b = dve_bank()
                    for hd in range(4):
                        mm = pe.transpose(ps[0:NCMP, b, hd * P:(hd + 1) * P], ec[:, tt * 4 + hd, :], ident[:, :])
                    mm.then_inc(dve_bank_full, 1)
                    t.next(dve_bank_full)
                emptied()
                for tt in range(TT):
                    b = dve_bank()
                    for hd in range(4):
                        mm = pe.matmul(ps[:, b, hd * DH:(hd + 1) * DH], ecT[0:NCMP, tt * 4 + hd, :],
                                       vg[0:NCMP, :], start=True, stop=True)
                    mm.then_inc(dve_bank_full, 1)
                    t.next(dve_bank_full)
            afresh()
            turn_heads(KD)
            for j in range(2):
                project(hT, MOE_FIRST - 4 + j, 512, (dve_bank_full, dve_bank_full))
            cross(1, MOE_FIRST - 2)

            turn_h()
            b = dve_bank()
            for tt in range(TT):
                for k in range(KD):
                    mm = pe.matmul(ps[:, b, tt * NE:(tt + 1) * NE], hT[:, k, tt * P:(tt + 1) * P], rw[:, k, :],
                                   start=(k == 0), stop=(k == KD - 1))
                    if tt == k == 0:
                        mm.then_inc(weights_used, 1)
            mm.then_inc(dve_bank_full, 1)
            t.next(dve_bank_full)
            pe.wait_ge(members_ready, t.next(members_ready))
            b = dve_bank()
            pe.matmul(ps[:, b, 0:NE], before[:, :], member[:, 0, :], start=True, stop=True)
            pe.matmul(ps[:, b, NE:2 * NE], ones[:, :], member[:, 0, :], start=True, stop=False)
            pe.matmul(ps[:, b, NE:2 * NE], before[:, :], member[:, 1, :], start=False, stop=True)
            pe.matmul(ps[:, b, 2 * NE:3 * NE], ones[:, :], member[:, 0, :], start=True, stop=False)
            pe.matmul(ps[:, b, 2 * NE:3 * NE], ones[:, :], member[:, 1, :], start=False, stop=True).then_inc(dve_bank_full, 1)
            t.next(dve_bank_full)
            emptied()
            pe.wait_ge(probs_ready, t.value(scores_ready))

            def gather():
                pe.wait_ge(sel_ready, t.next(sel_ready))
                for k in range(KD):
                    for tt in range(TT):
                        mm = pe.matmul(ps[:, 2 + k // 4, (k % 4) * P:(k % 4 + 1) * P], h[:, tt, k * P:(k + 1) * P],
                                       sel[:, tt, :], start=(tt == 0), stop=(tt == TT - 1))
                mm.then_inc(gathered, 1)
                t.next(gathered)

            def scatter():
                pe.wait_ge(down_saved, t.next(down_saved))
                pe.wait_ge(selT_ready, t.value(selT_full) + 1)
                for tt in range(TT):
                    for c in range(2):
                        mm = pe.matmul(ps[:, (2, 3, 6, 7)[2 * tt + c], :], selT[:, tt * P:(tt + 1) * P],
                                       outE[:, c * 512:(c + 1) * 512], start=True, stop=True)
                mm.then_inc(scattered, 1)
                t.next(scattered)

            def part(terms, bnks, first_, last):
                pe.wait_ge(lo_ready, t.next(lo_ready))
                st = part.k % STAGES
                part.k += 1
                for (hi, lo, at), bnk in zip(terms, bnks):
                    w_h, w_l = w_hi[:, st, at:at + 512], w_lo[:, st, at:at + 512]
                    pe.matmul(ps[:, bnk, :], hi, w_h, start=first_ and (bnk != part.open), stop=False, skip_group_check=True)
                    part.open = bnk
                    pe.matmul(ps[:, bnk, :], lo, w_h, start=False, stop=False, skip_group_check=True)
                    mm = pe.matmul(ps[:, bnk, :], hi, w_l, start=False, stop=last, skip_group_check=True)
                mm.then_inc(part_used, 1)
                t.next(part_used)
            part.k = 0

            def e_wide(bnk):
                for q in range(PARTS):
                    part.open = None
                    part([(x_hi[:, 2 * q + n, :], x_lo[:, 2 * q + n, :], n * 512) for n in range(2)], (bnk, bnk),
                         q == 0, q == PARTS - 1)

            def e_down(first_, last):
                for q in range(PARTS):
                    part.open = None
                    part([(a_hi[:, q, :], a_lo[:, q, :], c * 512) for c in range(2)], (0, 1), first_ and q == 0,
                         last and q == PARTS - 1)

            def e_turn():
                pe.wait_ge(e_act_ready, t.next(e_act_ready))
                for kc in range(4):
                    mm = pe.transpose(ps[:, 6, kc * P:(kc + 1) * P], e_act[:, kc * P:(kc + 1) * P], ident[:, :])
                mm.then_inc(e_turned, 1)
                t.next(e_turned)

            for c in range(STAGES):
                pe.matmul(ps[:, c // 2, (c % 2) * 256:(c % 2 + 1) * 256], zeros[:, 0:P], zeros[:, :],
                          start=True, stop=True).then_inc(part_used, 1)
                t.next(part_used)
            pe.wait_ge(routed, 1)
            n_it = pe.value_load(rounds[0:1, 0:1], min_val=NE, max_val=2 * NE)
            gather()
            with t.loop(pe, 0, n_it, {lo_ready: NPARTS, part_used: NPARTS, e_act_ready: ESTEPS, e_turned: ESTEPS,
                                      sel_ready: 1, gathered: 1, scattered: 1, added: 1, selT_full: 1,
                                      down_saved: 1}) as it:
                pe.wait_ge(x_hi_ready, t.value(gathered))
                pe.wait_ge(x_lo_ready, t.value(gathered))
                for s in range(ESTEPS):
                    e_wide(4)
                    e_wide(5)
                    if s == 0:
                        scatter()
                        pe.wait_ge(added, t.next(added))
                    else:
                        pe.wait_ge(a_hi_ready, t.value(e_turned))
                        pe.wait_ge(a_lo_ready, t.value(e_turned))
                        e_down(s == 1, False)
                    if s < ESTEPS - 1:
                        e_turn()
                pe.wait_ge(e_act_ready, t.value(e_act_ready) + 1)
                for tt in range(TT):
                    mm = pe.transpose(ps[:, 7, tt * P:(tt + 1) * P], selg[:, tt, :], ident[:, :])
                mm.then_inc(selT_full, 1)
                t.next(selT_full)
                e_turn()
                gather()
                pe.wait_ge(a_hi_ready, t.value(e_turned))
                pe.wait_ge(a_lo_ready, t.value(e_turned))
                e_down(False, True)
            pe.wait_ge(x_hi_ready, t.value(gathered))
            pe.wait_ge(x_lo_ready, t.value(gathered))
            scatter()

        @block.scalar
        def _(sc_):
            t = Tally()

            def step(ins):
                ins.then_inc(act_step, 1)
                sc_.wait_ge(act_step, t.next(act_step))

            def bank():
                k = bank.k
                bank.k += 1
                sc_.wait_ge(act_bank_full, t.next(act_bank_full))
                return k % 2
            bank.k = 0

            def freed(ins):
                ins.then_inc(act_bank_free, 1)
                t.next(act_bank_free)

            def own_evacs():
                sc_.wait_ge(act_bank_free, t.value(act_bank_free))

            def norm():
                sc_.wait_ge(x_ready, t.next(x_ready))
                for tt in range(TT):
                    ins = sc_.activation(h[:, tt, :], (mem_x if norm.mem else xs)[:, tt, :], ACT.Square, accum_out=ss[:, tt:tt + 1])
                step(ins)
                sc_.activation(rms[:, :], ss[:, :], ACT.Sqrt, scale=1.0 / D, bias=eps[:, 0:1]).then_inc(rms_ready, 1)
            norm.mem = False

            def turn_h(gain):
                for j in (0, 2):
                    b = bank()
                    for n in range(2):
                        ins = sc_.activation(hT[:, 2 * j + n, :], ps[:, b, n * S:(n + 1) * S], ACT.Copy,
                                             scale=gT[:, gain, 2 * j + n:2 * j + n + 1])
                    freed(ins)

            def turn_heads(at, n):
                for j in range(0, n // 2, 2):
                    b = bank()
                    freed(sc_.activation(hT[:, at + 2 * j:at + 2 * j + 2, :].rearrange("p k s -> p (k s)"), ps[:, b, :], ACT.Copy))

            def save(dst, n):
                b = bank()
                freed(sc_.activation(dst, ps[:, b, 0:n], ACT.Copy))

            def attend(is_causal):
                for tt in range(TT):
                    keys = P if is_causal and tt == 0 else S
                    for par in range(2):
                        sc_.wait_ge(nmax_ready, t.next(nmax_ready))
                        for j in range(2):
                            hd = 2 * j + par
                            c = tt * 4 + hd
                            ins = sc_.activation(prob[:, tt, hd, 0:keys], ps[:, 2 + par, j * keys:(j + 1) * keys], ACT.Exp,
                                                 bias=nmax[:, c:c + 1], accum_out=rsum[:, c:c + 1])
                        ins.then_inc(probs_ready, 1)
                for j in range(3 if is_causal else 4):
                    if j % 2:
                        b = bank()
                        freed(sc_.activation(pT[:, j, :], ps[:, b, :], ACT.Copy))

            def afresh():
                bank.k = 0

            def cross(layer):
                norm()
                turn_h(3 * layer + 1)
                save(qr[:, 0, :], 256)
                b = bank()
                freed(sc_.activation(qT[:, :, :].rearrange("p a s -> p (a s)"), ps[:, b, :], ACT.Copy, scale=SCALE))
                attend(False)
                turn_heads(0, 2)

            sc_.dma_start(mem_x, mem[0].rearrange("(t p) d -> p t d", p=P)).then_inc(mem_loaded, 16)
            rows_at = 0
            for src in (norm_g.rearrange("l n (k p) -> (l n k) p", p=P), mem_g.rearrange("(k p) -> k p", p=P),
                        pool_scale[0].rearrange("(k p) -> k p", p=P),
                        cmp_pe_k[0].rearrange("(j r) d -> j (r d)", r=2), cmp_pe_v[0].rearrange("(j r) d -> j (r d)", r=2)):
                sc_.dma_start(small_rows[rows_at:rows_at + src.shape[0], :], src).then_inc(rows_loaded, 16)
                rows_at += src.shape[0]
            assert rows_at == NROWS
            sc_.dma_start(xs[:, :, :], x[0].rearrange("(t p) d -> p t d", p=P)).then_inc(x_loaded, 16)
            with nc.allow_non_contiguous_dma(reason="small"):
                sc_.dma_start(pos_i[:, :], positions.rearrange("(t p) -> p t", p=P)).then_inc(small_loaded, 16)
                for j in range(2):
                    sc_.dma_start(pw[j * DH:(j + 1) * DH, :, :],
                                  pool_w[0].rearrange("(r j) c d -> j c r d", j=2)[j]).then_inc(small_loaded, 16)
                sc_.dma_start(rw[:, :, :], router_w[0].rearrange("(k p) e -> p k e", p=P)).then_inc(small_loaded, 16)
                for v, w_ in enumerate((cmp_k_w2, cmp_v_w2)):
                    sc_.dma_start(w2[:, v, :, :], w_[0].rearrange("(k p) d -> p k d", p=P)).then_inc(late_loaded, 16)

            norm.mem = True
            sc_.wait_ge(mem_loaded, 16)
            sc_.wait_ge(consts_ready, 1)
            norm()
            norm.mem = False
            sc_.wait_ge(small_ready, 1)
            turn_h(6)
            for layer in range(2):
                save(kvm[:, layer, 0, :], 512)
            sc_.wait_ge(x_loaded, 16)
            norm()
            turn_h(0)
            for j in range(5):
                save(u[:, 0, 512 * j:512 * (j + 1)], 512)
            sc_.wait_ge(angles_ready, t.next(angles_ready))
            sc_.activation(sin[:, :, :], red[:, 0], ACT.Sin).then_inc(tables_ready, 1)
            sc_.activation(cos[:, :, :], red[:, 1], ACT.Sin, scale=-1.0, bias=half_pi[:, 0:1]).then_inc(tables_ready, 1)
            sc_.wait_ge(u_ready, t.next(u_ready))
            afresh()
            with t.loop(sc_, 0, MOBA_UNITS, {act_bank_full: 2, act_bank_free: 2, nmax_ready: 4, heads_ready: 1}) as i:
                sc_.activation(qr[:, :, :], u[:, :, bass.ds(i * 256 + POOL, 256)], ACT.Copy).then_inc(act_staged, 1)
                b = bank()
                freed(sc_.activation(qT[:, :, :].rearrange("p a s -> p (a s)"), ps[:, b, :], ACT.Copy, scale=SCALE))
                attend(True)
                sc_.wait_ge(heads_ready, t.next(heads_ready))
            afresh()
            turn_heads(2, MOBA // P)
            t.next(heads_ready)
            cross(0)
            t.next(heads_ready)
            norm()
            turn_h(2)

            sc_.wait_ge(hT_stands, 1)
            own_evacs()
            for k in range(0, KD, 2):
                sc_.activation(h_hi[:, k:k + 2, :], hT[:, k:k + 2, :], ACT.Copy).then_inc(h_hi_ready, 1)

            def f_high(slot, parts, loads):
                s_ = weights_ready[slot % RING]
                sc_.wait_ge(s_, t.next(s_, 16 * loads))
                for q in range(parts):
                    n = t.value(f_hi_ready)
                    if t.i is not None or n >= F_STAGES:
                        sc_.wait_ge(f_part_used, n - F_STAGES + 1)
                    sc_.activation(f_w_hi[:, f_high.k % F_STAGES, :], raw(slot % RING, q), ACT.Copy).then_inc(f_hi_ready, 1)
                    t.next(f_hi_ready)
                    f_high.k += 1
            f_high.k = 0

            def silus():
                for tt in range(TT):
                    sc_.activation(sgate[:, tt * FSTEP:(tt + 1) * FSTEP], ps[:, 4 + tt, 0:FSTEP], ACT.Silu).then_inc(silu_ready, 1)

            def save_turned():
                sc_.wait_ge(turned, t.next(turned))
                sc_.activation(aT_hi[:, :], ps[:, 6, :], ACT.Copy).then_inc(aT_hi_ready, 1)

            t.n.update({w.name: head_loads.get(w.name, 0) for w in weights_ready})
            f_high(FFN_FIRST, PARTS, 2)
            sc_.wait_ge(f_part_used, PARTS)
            silus()
            per = {weights_ready[(FFN_LOOP + j) % RING]: (32, 16)[j % 2] for j in range(4)}
            with t.loop(sc_, 0, (FSTEPS - 1) // 2, {**per, f_hi_ready: 12, turned: 2}) as i:
                for j in range(2):
                    f_high(FFN_LOOP + 2 * j, PARTS, 2)
                    save_turned()
                    f_high(FFN_LOOP + 2 * j + 1, 2, 1)
                    sc_.wait_ge(f_part_used, t.value(f_hi_ready) - 2)
                    silus()
            save_turned()
            f_high(FFN_LAST, 2, 1)
            norm()
            turn_h(3)
            for j, (c0, n) in enumerate(IN_C):
                save(u[:, 0, c0:c0 + n], n)
            sc_.wait_ge(u_ready, t.next(u_ready))
            own_evacs()
            sc_.activation(sg[:, :, :], u[:, :, GL0:GL0 + 48], ACT.Sigmoid).then_inc(gates_ready, 1)
            b = bank()
            freed(sc_.activation(KTp[:, 0:2, :].rearrange("p a b -> p (a b)"), ps[:, b, :], ACT.Copy))
            own_evacs()
            for v in range(2):
                if v == 1:
                    sc_.wait_ge(vcT_ready, 1)
                for par in range(2):
                    src = KTp[par * DH:(par + 1) * DH, 2 * v:2 * v + 2, :]
                    sc_.dma_start(KT2[0:DH, v, par:GROUPS:2, :], src).then_inc(shifted[4 * v + 2 * par], 16)
                    sc_.dma_start(KT2[DH:P, v, par:GROUPS:2, 0:S - 1], src[:, :, 1:S]).then_inc(shifted[4 * v + 2 * par + 1], 16)
            for v in range(2):
                b = bank()
                freed(sc_.activation(hid[0:GROUPS * NCMP, v, :], ps[0:GROUPS * NCMP, b, 0:CMP_HID], ACT.Gelu_apprx_tanh))
            afresh()
            with t.loop(sc_, 0, GROUPS, {act_bank_full: 4, act_bank_free: 4, nmax_ready: 8, heads_ready: 1, cmp_shifted: 1}) as g:
                sc_.activation(qc[:, :, :], u[:, :, bass.ds(g * 256, 256)], ACT.Copy)
                for tt in range(TT):
                    ins = sc_.activation(qr[:, tt, :].rearrange("p (h d) -> p h d", h=4)[:, :, ROPE:DH],
                                         u[:, tt, bass.ds(g * 256, 256)].rearrange("p (h d) -> p h d", h=4)[:, :, ROPE:DH],
                                         ACT.Copy)
                ins.then_inc(act_staged, 1)
                for dst in (qT, qcT):
                    b = bank()
                    freed(sc_.activation(dst[:, :, :].rearrange("p a s -> p (a s)"), ps[:, b, :], ACT.Copy, scale=SCALE))
                sc_.wait_ge(cmp_shifted, t.next(cmp_shifted))
                sc_.activation(ec[:, :, :], sc[:, :, :], ACT.Exp).then_inc(cmp_exp, 1)
                attend(True)
                attend(True)
                sc_.wait_ge(heads_ready, t.next(heads_ready))
            afresh()
            turn_heads(0, KD)
            t.next(heads_ready)
            cross(1)
            norm()
            turn_h(5)
            sc_.wait_ge(gap_ready, t.next(gap_ready))
            sc_.activation(gap[:, 1, :], gap[:, 0, :], ACT.Exp).then_inc(gap_exp, 1)
            sc_.wait_ge(routed, 1)
            n_it = sc_.value_load(rounds[0:1, 0:1], min_val=NE, max_val=2 * NE)

            def high(unit):
                slot = SLOTS[unit]
                for q in range(PARTS):
                    if q == 0:
                        sc_.wait_ge(weights_ready[slot], t.next(weights_ready[slot], 16))
                    sc_.wait_ge(part_used, t.value(hi_ready) + 1)
                    sc_.activation(w_hi[:, high.k % STAGES, :], raw(slot, q), ACT.Copy).then_inc(hi_ready, 1)
                    t.next(hi_ready)
                    high.k += 1
            high.k = 0

            def save_x():
                sc_.wait_ge(gathered, t.next(gathered))
                sc_.activation(x_hi[:, :, :].rearrange("p (b a) c -> p b (a c)", b=2), ps[:, 2:4, :], ACT.Copy).then_inc(x_hi_ready, 1)

            def save_down():
                sc_.activation(outE[:, :].rearrange("p (c n) -> p c n", c=2), ps[:, 0:2, :], ACT.Copy).then_inc(down_saved, 1)

            def e_save_turned():
                sc_.wait_ge(e_turned, t.next(e_turned))
                sc_.activation(a_hi[:, :, :].rearrange("p a b -> p (a b)"), ps[:, 6, :], ACT.Copy).then_inc(a_hi_ready, 1)

            t.n.update({w.name: trunk_loads[w.name] for w in weights_ready})
            sc_.activation(selT[:, :], zeros[:, :], ACT.Copy).then_inc(selT_ready, 1)
            save_x()
            with t.loop(sc_, 0, n_it, {**{w: 48 for w in weights_ready}, hi_ready: NPARTS, e_turned: ESTEPS,
                                       selT_full: 1, gathered: 1}) as it:
                for s in range(ESTEPS):
                    high(("g", s))
                    if s == 0:
                        sc_.wait_ge(part_used, t.value(hi_ready) - PARTS + STAGES)
                        save_down()
                    else:
                        e_save_turned()
                    high(("u", s))
                    sc_.wait_ge(part_used, t.value(hi_ready) - PARTS + STAGES)
                    sc_.activation(e_gate[:, :], ps[:, 4, :], ACT.Silu).then_inc(e_silu_ready, 1)
                    if s:
                        high(("d", s - 1))
                high(("d", ESTEPS - 1))
                sc_.wait_ge(selT_full, t.next(selT_full))
                sc_.activation(selT[:, :], ps[:, 7, 0:S], ACT.Copy).then_inc(selT_ready, 1)
                e_save_turned()
                save_x()
            sc_.wait_ge(part_used, t.value(hi_ready) + STAGES)
            save_down()
            norm()

        @block.vector
        def _(ve):
            t = Tally()

            def step(ins):
                ins.then_inc(dve_step, 1)
                ve.wait_ge(dve_step, t.next(dve_step))

            def bank():
                k = bank.k
                bank.k += 1
                ve.wait_ge(dve_bank_full, t.next(dve_bank_full))
                return 6 + k % 2
            bank.k = 0

            def freed(ins):
                ins.then_inc(dve_bank_free, 1)
                t.next(dve_bank_free)

            def own_evacs():
                ve.wait_ge(dve_bank_free, t.value(dve_bank_free))

            def norm(src):
                ve.wait_ge(rms_ready, t.next(rms_ready))
                step(ve.reciprocal(rstd[:, :], rms[:, :]))
                for tt in range(TT):
                    ins = ve.tensor_scalar(h[:, tt, :], src[:, tt, :], rstd[:, tt:tt + 1], None, ALU.mult)
                ins.then_inc(h_ready, 1)
                t.next(h_ready)

            def x_stands():
                own_evacs()
                ve.nop().then_inc(x_ready, 1)

            def turn_h(gain):
                for j in (1, 3):
                    b = bank()
                    for n in range(2):
                        ins = ve.tensor_scalar(hT[:, 2 * j + n, :], ps[:, b, n * S:(n + 1) * S],
                                               gT[:, gain, 2 * j + n:2 * j + n + 1], None, ALU.mult)
                    freed(ins)

            def turn_heads(at, n):
                for j in range(1, n // 2, 2):
                    b = bank()
                    freed(ve.tensor_copy(hT[:, at + 2 * j:at + 2 * j + 2, :].rearrange("p k s -> p (k s)"), ps[:, b, :]))

            def save(dst, n):
                b = bank()
                freed(ve.tensor_copy(dst, ps[:, b, 0:n]))

            def add_x(tt, c):
                b = bank()
                part = xs[:, tt, c * 512:(c + 1) * 512]
                freed(ve.tensor_tensor(part, ps[:, b, :], part, ALU.add))

            def heads_stand():
                own_evacs()
                ve.nop().then_inc(heads_ready, 1)

            def attend(is_causal, result):
                for tt in range(TT):
                    keys = P if is_causal and tt == 0 else S
                    for par in range(2):
                        ve.wait_ge(scores_ready, t.next(scores_ready))
                        ve.tensor_reduce(nmax[:, 4 * tt + par:4 * tt + 4:2],
                                         ps[:, 2 + par, 0:2 * keys].rearrange("p (h k) -> p h k", h=2), AX, ALU.max,
                                         negate=True).then_inc(nmax_ready, 1)
                for j in range(3 if is_causal else 4):
                    if j % 2 == 0:
                        b = bank()
                        freed(ve.tensor_copy(pT[:, j, :], ps[:, b, :]))
                for tt in range(TT):
                    b = bank()
                    if tt == 0:
                        step(ve.reciprocal(rinv[:, :], rsum[:, :]))
                    result(tt, b)

            def afresh():
                bank.k = 0

            def per_head(v, n=4):
                return v.rearrange("p (h d) -> p h d", h=n)

            def wide_of(c, n):
                return c.unsqueeze(2).to_broadcast([P, n, DH])

            def rotate(lo, hi, out_lo, out_hi, n):
                c = cos[:, :, :].unsqueeze(2).to_broadcast([P, TT, n, HALF])
                s = sin[:, :, :].unsqueeze(2).to_broadcast([P, TT, n, HALF])
                r = [rt[:, j, :, 0:n, :] for j in range(4)]
                ve.tensor_tensor(r[0], lo, c, ALU.mult)
                ve.tensor_tensor(r[1], hi, s, ALU.mult)
                ve.tensor_tensor(r[2], lo, s, ALU.mult)
                step(ve.tensor_tensor(r[3], hi, c, ALU.mult))
                ve.tensor_tensor(out_lo, r[0], r[1], ALU.subtract)
                step(ve.tensor_tensor(out_hi, r[2], r[3], ALU.add))

            def cross(layer):
                norm(xs)
                turn_h(3 * layer + 1)
                save(qr[:, 1, :], 256)
                save(kT[:, :, :].rearrange("p a s -> p (a s)"), 512)

                def result(tt, b):
                    freed(ve.tensor_tensor(per_head(h[:, tt, 0:256]), per_head(ps[:, b, 0:256]),
                                           wide_of(rinv[:, 4 * tt:4 * tt + 4], 4), ALU.mult))
                attend(False, result)
                heads_stand()
                turn_heads(0, 2)
                for tt in range(TT):
                    for c in range(2):
                        add_x(tt, c)
                x_stands()

            ve.wait_ge(mem_loaded, 16)
            ve.nop().then_inc(x_ready, 1)
            norm(mem_x)
            b = bank()
            ve.tensor_copy(small[:, :], ps[:, b, 0:NROWS]).then_inc(small_ready, 1)
            ve.wait_ge(small_ready, 1)
            freed(ve.nop())
            turn_h(6)
            for layer in range(2):
                save(kvm[:, layer, 1, :], 512)
            own_evacs()
            ve.wait_ge(x_loaded, 16)
            ve.nop().then_inc(x_ready, 1)
            norm(xs)
            turn_h(0)
            ve.wait_ge(small_loaded, 16 * 4)
            step(ve.tensor_copy(pos[:, :], pos_i[:, :]))
            for j in range(HALF):
                inv = float(np.float32(np.float32(THETA) ** np.float32(-2.0 * j / ROPE)))
                ins = ve.tensor_scalar(ang[:, :, j], pos[:, :], inv, None, ALU.mult)
            step(ins)
            step(ve.tensor_scalar(red[:, 1], ang[:, :, :], 1.0 / (2 * math.pi), MAGIC, ALU.mult, ALU.add))
            step(ve.tensor_scalar(red[:, 1], red[:, 1], MAGIC, None, ALU.subtract))
            prev = ang[:, :, :]
            for part in (*TWO_PI, TWO_PI_REST):
                step(ve.scalar_tensor_tensor(red[:, 0], red[:, 1], -part, prev, ALU.mult, ALU.add))
                prev = red[:, 0]
            step(ve.tensor_scalar(red[:, 0], red[:, 0], math.pi - 1e-6, -(math.pi - 1e-6), ALU.min, ALU.max))
            step(ve.tensor_scalar(red[:, 1], red[:, 0], -1.0, None, ALU.mult))
            ve.tensor_tensor(red[:, 1], red[:, 1], red[:, 0], ALU.max).then_inc(angles_ready, 1)
            ve.wait_ge(band_counted, 1)
            for j in range(5):
                save(u[:, 1, 512 * j:512 * (j + 1)], 512)
                if j < 4:
                    ins = ve.reciprocal(band[:, j, :, :], band[:, j, :, :])
                    if j == 3:
                        ins.then_inc(counts_ready, 1)
            own_evacs()
            ve.wait_ge(consts_ready, 2)
            ve.wait_ge(late_loaded, 16 * 2)
            ve.wait_ge(act_bank_free, 2 + 2 + 2 + 5)
            for pr in range(2):
                save(pooled[:, pr, :], S)
            for pr in range(2):
                b = bank()
                freed(ve.tensor_scalar(hT[:, pr, :], ps[:, b, 0:S], pscale[:, pr:pr + 1], None, ALU.mult))
            ve.wait_ge(tables_ready, 2)
            qk = u[:, :, POOL:POOL + 2 * MOBA].rearrange("p t (h d) -> p t h d", d=DH)
            rotate(qk[:, :, :, 0:HALF], qk[:, :, :, HALF:ROPE], qk[:, :, :, 0:HALF], qk[:, :, :, HALF:ROPE], 2 * MOBA // DH)
            ve.nop().then_inc(u_ready, 1)
            afresh()
            with t.loop(ve, 0, MOBA_UNITS, {dve_bank_full: 5, dve_bank_free: 5, dve_step: 1, scores_ready: 4}) as i:
                ve.tensor_copy(kk[:, :, :], u[:, :, bass.ds(i * 256 + (POOL + MOBA), 256)]).then_inc(dve_staged, 1)
                save(kT[:, :, :].rearrange("p a s -> p (a s)"), 512)

                def result(tt, b):
                    freed(ve.tensor_tensor(per_head(h[:, tt, bass.ds(i * 256, 256)]), per_head(ps[:, b, 0:256]),
                                           wide_of(rinv[:, 4 * tt:4 * tt + 4], 4), ALU.mult))
                attend(True, result)
                heads_stand()
            afresh()
            heads_stand()
            turn_heads(2, MOBA // P)
            for c in range(2):
                for tt in range(TT):
                    add_x(tt, c)
            x_stands()
            cross(0)
            norm(xs)
            turn_h(2)

            own_evacs()
            ve.nop().then_inc(hT_stands, 1)
            for k in range(0, KD, 2):
                ve.wait_ge(h_hi_ready, k // 2 + 1)
                ve.tensor_tensor(h_lo[:, k:k + 2, :], hT[:, k:k + 2, :], h_hi[:, k:k + 2, :].bitcast(F32),
                                 ALU.subtract).then_inc(h_lo_ready, 1)

            def f_low(slot, parts):
                for q in range(parts):
                    ve.wait_ge(f_hi_ready, t.next(f_hi_ready))
                    st = f_low.k % F_STAGES
                    ve.tensor_tensor(f_w_lo[:, st, :], raw(slot % RING, q), f_w_hi[:, st, :].bitcast(F32), ALU.subtract).then_inc(f_lo_ready, 1)
                    f_low.k += 1
            f_low.k = 0

            def times_up():
                for tt in range(TT):
                    ve.wait_ge(silu_ready, t.next(silu_ready))
                    part = slice(tt * FSTEP, (tt + 1) * FSTEP)
                    ve.tensor_tensor(act[:, part], ps[:, 4 + tt, FSTEP:2 * FSTEP], sgate[:, part], ALU.mult).then_inc(act_ready, 1)

            def save_turned():
                ve.wait_ge(aT_hi_ready, t.next(aT_hi_ready))
                ve.tensor_tensor(aT_lo[:, :], ps[:, 6, :], aT_hi[:, :].bitcast(F32), ALU.subtract).then_inc(aT_lo_ready, 1)

            f_low(FFN_FIRST, PARTS)
            times_up()
            with t.loop(ve, 0, (FSTEPS - 1) // 2, {f_hi_ready: 12, silu_ready: 4, aT_hi_ready: 2}) as i:
                for j in range(2):
                    f_low(FFN_LOOP + 2 * j, PARTS)
                    save_turned()
                    f_low(FFN_LOOP + 2 * j + 1, 2)
                    times_up()
            save_turned()
            f_low(FFN_LAST, 2)
            ve.wait_ge(f_part_used, PARTS + 6 * (FSTEPS - 1) + 2)
            for tt in range(TT):
                part = xs[:, tt, :].rearrange("p (c n) -> p c n", c=2)
                ins = ve.tensor_tensor(part, ps[:, 2 * tt:2 * tt + 2, :], part, ALU.add)
            ins.then_inc(ffn_added, 1)
            ve.wait_ge(ffn_added, 1)
            ve.nop().then_inc(x_ready, 1)
            norm(xs)
            turn_h(3)
            for j, (c0, n) in enumerate(IN_C):
                save(u[:, 1, c0:c0 + n], n)
            own_evacs()
            ve.nop().then_inc(u_ready, 1)
            save(KTp[:, 2:4, :].rearrange("p a b -> p (a b)"), 512)
            own_evacs()
            ve.nop().then_inc(vcT_ready, 1)
            ve.wait_ge(gates_ready, 1)
            for c0, n, olo, ohi in ((0, 16, rq[:, :, :, 0:HALF], rq[:, :, :, HALF:ROPE]), (KS0, 4, None, None), (KW0, 4, None, None)):
                v = u[:, :, c0:c0 + n * DH].rearrange("p t (h d) -> p t h d", d=DH)
                lo, hi = v[:, :, :, 0:HALF], v[:, :, :, HALF:ROPE]
                rotate(lo, hi, lo if olo is None else olo, hi if ohi is None else ohi, n)
            for v, X in enumerate((KX, VX)):
                for q in shifted[4 * v:4 * v + 4]:
                    ve.wait_ge(q, 16)
                src = KT2[:, v, :, :].rearrange("p g (n j r) -> p j g n r", j=8, r=2)[:, :, :, :, 0]
                for half in range(2):
                    for g in range(GROUPS):
                        ins = ve.tensor_tensor(X[:, 8 * half:8 * half + 8, g, :], src[:, :, g, half:half + NCMP],
                                               pe_kv[:, v, 8 * half:8 * half + 8].unsqueeze(2).to_broadcast([P, 8, NCMP]), ALU.add)
            ins.then_inc(cmp_in_ready, 1)
            b = bank()
            freed(ve.tensor_copy(hidT[:, :, :, :].rearrange("p v k n -> p (v k n)"), ps[:, b, 0:4 * GROUPS * NCMP]))
            save(kcmpT[:, :], GROUPS * NCMP)
            b = bank()
            freed(ve.tensor_copy(vcmp[0:NCMP, :, :].rearrange("p g d -> p (g d)"), ps[0:NCMP, b, 0:GROUPS * DH]))
            own_evacs()
            afresh()
            sgv = sg[:, :, :].rearrange("p t (h b) -> p t h b", b=3)
            with t.loop(ve, 0, GROUPS, {dve_bank_full: 15, dve_bank_free: 15, dve_step: 13, scores_ready: 8, cmp_exp: 1}) as g:
                for half in range(2):
                    for tt in range(TT):
                        ve.tensor_copy(kk[:, tt, half * P:(half + 1) * P].rearrange("p (r d) -> p r d", r=2),
                                       u[:, tt, bass.ds(g * DH + (KS0, KW0)[half], DH)].unsqueeze(1).to_broadcast([P, 2, DH]))
                ve.tensor_copy(kcT[:, 0:NCMP], kcmpT[:, bass.ds(g * NCMP, NCMP)])
                ve.tensor_copy(vg[0:NCMP, :], vcmp[0:NCMP, bass.ds(g, 1), :].rearrange("p g d -> p (g d)"))
                for tt in range(TT):
                    ins = ve.tensor_copy(per_head(qr[:, tt, :])[:, :, 0:ROPE], rq[:, tt, bass.ds(g * 4, 4), :])
                ins.then_inc(dve_staged, 1)
                save(kT[:, :, :].rearrange("p a s -> p (a s)"), 512)
                sc4 = sc[:, :, :].rearrange("p (t h) n -> p t h n", t=TT)
                for par in range(2):
                    b = bank()
                    freed(ve.tensor_tensor(sc4[:, :, par:4:2, :],
                                           ps[:, b, 0:64].rearrange("p (t h n) -> p t h n", t=TT, h=2)[:, :, :, 0:NCMP],
                                           cmask[:, :, :].unsqueeze(2).to_broadcast([P, TT, 2, NCMP]), ALU.add))
                own_evacs()
                step(ve.tensor_reduce(cmx[:, 0, :], sc[:, :, :], AX, ALU.max))
                step(ve.tensor_scalar(cmx[:, 0, :], cmx[:, 0, :], -CLAMP, None, ALU.max))
                ve.tensor_tensor(sc[:, :, :], sc[:, :, :], cmx[:, 0, :].unsqueeze(2).to_broadcast([P, 8, NCMP]),
                                 ALU.subtract).then_inc(cmp_shifted, 1)

                def weights(inv, branch):
                    step(ve.tensor_tensor(coef[:, :].rearrange("p (t h) -> p t h", t=TT), inv.rearrange("p (t h) -> p t h", t=TT),
                                          sgv[:, :, bass.ds(g * 4, 4), branch], ALU.mult))

                def result_of(branch, into):
                    def result(tt, b):
                        if tt == 0:
                            weights(rinv[:, :], branch)
                        freed(ve.tensor_tensor(per_head(into[:, tt, :]), per_head(ps[:, b, 0:256]),
                                               wide_of(coef[:, 4 * tt:4 * tt + 4], 4), ALU.mult))
                    return result
                attend(True, result_of(1, yg))
                attend(True, result_of(2, yt))
                own_evacs()
                step(ve.tensor_tensor(yg[:, :, :], yg[:, :, :], yt[:, :, :], ALU.add))
                ve.wait_ge(cmp_exp, t.next(cmp_exp))
                step(ve.tensor_reduce(cmx[:, 1, :], ec[:, :, :], AX, ALU.add))
                step(ve.tensor_scalar(cmx[:, 1, :], cmx[:, 1, :], 1e-30, None, ALU.max))
                step(ve.reciprocal(cmx[:, 1, :], cmx[:, 1, :]))
                weights(cmx[:, 1, :], 0)
                for tt in range(TT):
                    b = bank()
                    freed(ve.tensor_copy(ecT[0:NCMP, 4 * tt:4 * tt + 4, :].rearrange("p h s -> p (h s)"), ps[0:NCMP, b, :]))
                for tt in range(TT):
                    b = bank()
                    step(ve.tensor_tensor(per_head(yt[:, tt, :]), per_head(ps[:, b, 0:256]), wide_of(coef[:, 4 * tt:4 * tt + 4], 4), ALU.mult))
                    freed(ve.tensor_tensor(h[:, tt, bass.ds(g * 256, 256)], yg[:, tt, :], yt[:, tt, :], ALU.add))
                heads_stand()
            afresh()
            heads_stand()
            turn_heads(0, KD)
            for c in range(2):
                for tt in range(TT):
                    add_x(tt, c)
            x_stands()
            cross(1)

            norm(xs)
            turn_h(5)
            b = bank()
            freed(ve.tensor_copy(logit[:, :, :].rearrange("p t e -> p (t e)"), ps[:, b, 0:TT * NE]))
            own_evacs()
            for tt in range(TT):
                step(ve.max(top[:, tt, :], logit[:, tt, :]))
                step(ve.max_index(topi[:, tt, :], top[:, tt, :], logit[:, tt, :]))
            ve.tensor_tensor(gap[:, 0, :], top[:, :, 1], top[:, :, 0], ALU.subtract).then_inc(gap_ready, 1)
            step(ve.tensor_copy(topf[:, :, :], topi[:, :, :]))
            for j in range(2):
                for tt in range(TT):
                    ins = ve.tensor_scalar(hot[:, j, tt, :], iota8, topf[:, tt, j:j + 1], None, ALU.is_equal)
            step(ins)
            ve.tensor_tensor(member[:, :, :], hot[:, 0], hot[:, 1], ALU.add).then_inc(members_ready, 1)
            ve.wait_ge(gap_exp, 1)
            step(ve.tensor_scalar(gap[:, 2, :], gap[:, 1, :], 1.0, None, ALU.add))
            step(ve.reciprocal(gap[:, 2, :], gap[:, 2, :]))
            step(ve.tensor_tensor(gap[:, 3, :], gap[:, 1, :], gap[:, 2, :], ALU.mult))
            for tt in range(TT):
                step(ve.tensor_scalar(gate[:, tt, 0:NE], hot[:, 0, tt, :], gap[:, 2, tt:tt + 1], None, ALU.mult))
                step(ve.scalar_tensor_tensor(gate[:, tt, 0:NE], hot[:, 1, tt, :], gap[:, 3, tt:tt + 1], gate[:, tt, 0:NE],
                                             ALU.mult, ALU.add))
            b = bank()
            for tt in range(TT):
                step(ve.scalar_tensor_tensor(rank[:, tt, 0:NE], ps[:, b, tt * NE:(tt + 1) * NE], 1.0, member[:, tt, :],
                                             ALU.add, ALU.mult))
            step(ve.tensor_scalar(rank[:, :, 0:NE], rank[:, :, 0:NE], -1.0, None, ALU.add))
            freed(ve.tensor_reduce(most[:, 0:1], ps[:, b, 2 * NE:3 * NE], AX, ALU.max))
            own_evacs()
            for j in range(1, 3):
                step(ve.tensor_scalar(rank[:, :, j * NE:(j + 1) * NE], rank[:, :, 0:NE], -float(P * j), None, ALU.add))
                step(ve.tensor_copy(gate[:, :, j * NE:(j + 1) * NE], gate[:, :, 0:NE]))
            step(ve.tensor_scalar(most[:, 1:2], most[:, 0:1], P + 0.5, float(NE), ALU.is_gt, ALU.mult))
            step(ve.tensor_scalar(most[:, 1:2], most[:, 1:2], float(NE), None, ALU.add))
            ve.tensor_copy(rounds[:, :], most[:, 1:2]).then_inc(routed, 1)
            ve.wait_ge(routed, 1)
            ve.wait_ge(gains_loaded, 16 * 2)
            for tt in range(TT):
                ins = ve.tensor_tensor(h[:, tt, :], h[:, tt, :], moe_g[:, :], ALU.mult)
            step(ins)
            n_it = ve.value_load(rounds[0:1, 0:1], min_val=NE, max_val=2 * NE)

            def choose(it):
                for tt in range(TT):
                    ins = ve.tensor_scalar(sel[:, tt, :], iota128[:, :], rank[:, tt, bass.ds(it, 1)], None, ALU.is_equal)
                ins.then_inc(sel_ready, 1)

            def low(unit):
                for q in range(PARTS):
                    ve.wait_ge(hi_ready, t.next(hi_ready))
                    st = low.k % STAGES
                    ve.tensor_tensor(w_lo[:, st, :], raw(SLOTS[unit], q), w_hi[:, st, :].bitcast(F32), ALU.subtract).then_inc(lo_ready, 1)
                    low.k += 1
            low.k = 0

            def save_x():
                ve.wait_ge(x_hi_ready, t.next(x_hi_ready))
                ve.tensor_tensor(x_lo[:, :, :].rearrange("p (b a) c -> p b (a c)", b=2), ps[:, 2:4, :],
                                 x_hi[:, :, :].rearrange("p (b a) c -> p b (a c)", b=2).bitcast(F32), ALU.subtract).then_inc(x_lo_ready, 1)

            def e_save_turned():
                ve.wait_ge(a_hi_ready, t.next(a_hi_ready))
                ve.tensor_tensor(a_lo[:, :, :].rearrange("p a b -> p (a b)"), ps[:, 6, :],
                                 a_hi[:, :, :].rearrange("p a b -> p (a b)").bitcast(F32), ALU.subtract).then_inc(a_lo_ready, 1)

            choose(0)
            save_x()

            def add_scattered():
                ve.wait_ge(scattered, t.next(scattered))
                for tt in range(TT):
                    part = xs[:, tt, :].rearrange("p (c n) -> p c n", c=2)
                    ins = ve.tensor_tensor(part, ps[:, (2, 6)[tt]:(2, 6)[tt] + 2, :], part, ALU.add)
                ins.then_inc(added, 1)
                t.next(added)

            with t.loop(ve, 0, n_it, {hi_ready: NPARTS, e_silu_ready: ESTEPS, a_hi_ready: ESTEPS, x_hi_ready: 1,
                                      scattered: 1, added: 1}) as it:
                for s in range(ESTEPS):
                    low(("g", s))
                    if s:
                        e_save_turned()
                    low(("u", s))
                    if s:
                        low(("d", s - 1))
                    if s == ESTEPS - 1:
                        for tt in range(TT):
                            ve.tensor_scalar(selg[:, tt, :], iota128[:, :], rank[:, tt, bass.ds(it, 1)],
                                             gate[:, tt, bass.ds(it, 1)], ALU.is_equal, ALU.mult)
                    ve.wait_ge(part_used, t.value(hi_ready) - (PARTS if s else 0) + STAGES)
                    ve.wait_ge(e_silu_ready, t.next(e_silu_ready))
                    ve.tensor_tensor(e_act[:, :], ps[:, 5, :], e_gate[:, :], ALU.mult).then_inc(e_act_ready, 1)
                    if s == 0:
                        add_scattered()
                choose(it + 1)
                low(("d", ESTEPS - 1))
                e_save_turned()
                save_x()
            add_scattered()
            ve.wait_ge(added, t.value(added))
            ve.nop().then_inc(x_ready, 1)
            norm(xs)
            ve.wait_ge(h_ready, t.value(h_ready))
            for tt in range(TT):
                ins = ve.tensor_tensor(h[:, tt, :], h[:, tt, :], fin_g[:, :], ALU.mult)
            ins.then_inc(out_ready, 1)


_INS = ["x", "mem", "positions", "norm_g", "mem_g", "final_g", "w_in_ab", "pool_w", "pool_scale", "w_out_ab",
        "ffn_w_gate", "ffn_w_up", "ffn_w_down", "w_in_c", "cmp_pe_k", "cmp_pe_v", "cmp_k_w1", "cmp_k_w2",
        "cmp_v_w1", "cmp_v_w2", "w_out_c", "router_w", "moe_w_gate", "moe_w_up", "moe_w_down", "xa_wq", "xa_wkv", "xa_wo"]


def kernel(**inputs):
    import numpy as _np
    import concourse.bacc as _bacc
    from concourse import mybir as _mybir
    from concourse.bass_utils import run_bass_kernel_spmd as _run

    nc = _bacc.Bacc("TRN2", target_bir_lowering=False, num_devices=1)
    arrays, args = {}, []
    for name in _INS:
        a = _np.ascontiguousarray(inputs[name])
        arrays[f"in_{name}"] = a
        args.append(nc.dram_tensor(f"in_{name}", a.shape, _mybir.dt.from_np(a.dtype), kind="ExternalInput").ap())
    o = nc.dram_tensor("out", (1, S, D), _mybir.dt.float32, kind="ExternalOutput").ap()
    build(nc, *args, o)
    r = _run(nc, [arrays], core_ids=[0])
    return r.results[0]["out"]
```
